# Optimizing a Trainium2 kernel written in Bass

```python
import math
import numpy as np
import jax
import jax.numpy as jnp
from jax import lax

D_MODEL = 1024
BATCH = 1
SEQ = 128
DEPTH = 2
DEC_BATCH = 1
DEC_SEQ = 256
PAST_LEN = 128

GRID_W = 64
HA = 4
DA = 64
HB = 4
DKB = 64
DVB = 128
RET_CHUNK = 64
HC = 4
DC = 128
NA_ROWS = 8
NA_COLS = 16
N_BRANCH = 3
BRANCH_W = 512
PEER_HEADS = 8
PEER_NKEYS = 128
PEER_DKEY = 256
PEER_TOPK = 16
PEER_N = PEER_NKEYS * PEER_NKEYS
PEER_TOKEN_BLOCK = 128
Q_BLOCK = 128
ROPE_BASE = 10000.0
EPS = 1e-6
IN_WIDTHS = (HA * 2 * DA, HA * 2 * DA, HA * 2 * DA, HB * DKB, HB * DKB, HB * DVB, 2 * HB * DVB,
             HC * DC, HC * DC, HC * DC, N_BRANCH * D_MODEL)
IN_TOTAL = sum(IN_WIDTHS)

kernel_name = "hybrid_diffusion_prefix_trunk"

def rms_norm(x, g):
    x32 = x.astype(jnp.float32)
    y = x32 * lax.rsqrt(jnp.mean(x32 * x32, axis=-1, keepdims=True) + EPS)
    return (y * g.astype(jnp.float32)).astype(x.dtype)

def split_heads(x, h):
    b, L, _ = x.shape
    return x.reshape(b, L, h, -1).transpose(0, 2, 1, 3)

def merge_heads(x):
    b, h, L, d = x.shape
    return x.transpose(0, 2, 1, 3).reshape(b, L, h * d)

def rotate(x, ang):
    x1, x2 = jnp.split(x, 2, axis=-1)
    cos = jnp.cos(ang).astype(x.dtype)
    sin = jnp.sin(ang).astype(x.dtype)
    return jnp.concatenate([x1 * cos - x2 * sin, x1 * sin + x2 * cos], axis=-1)

def rope_2d(x):
    L, d = x.shape[-2], x.shape[-1]
    half = d // 2
    t = jnp.arange(L)
    rows = (t // GRID_W).astype(jnp.float32)
    cols = (t % GRID_W).astype(jnp.float32)
    freqs = ROPE_BASE ** (-jnp.arange(0, half, 2, dtype=jnp.float32) / half)
    return jnp.concatenate([rotate(x[..., :half], rows[:, None] * freqs),
                            rotate(x[..., half:], cols[:, None] * freqs)], axis=-1)

def softmax_attn(q, k, v):
    b, h, lq, d = q.shape
    nb = lq // Q_BLOCK
    qb = q.reshape(b, h, nb, Q_BLOCK, d).transpose(2, 0, 1, 3, 4)
    scale = d ** -0.5

    def one(qi):
        s = jnp.einsum('bhqd,bhkd->bhqk', qi, k).astype(jnp.float32) * scale
        p = jax.nn.softmax(s, axis=-1).astype(v.dtype)
        return jnp.einsum('bhqk,bhkd->bhqd', p, v)

    o = lax.map(one, qb)
    return o.transpose(1, 2, 0, 3, 4).reshape(b, h, lq, v.shape[-1])

def neighbourhood_attn(q, k, v, kc, vc, bias_table):
    b, h, L, d = q.shape
    rows = L // GRID_W
    kr = min(NA_ROWS, rows)
    scale = d ** -0.5
    qg = q.reshape(b, h, rows, GRID_W, d)
    kg = k.reshape(b, h, rows, GRID_W, d)
    vg = v.reshape(b, h, rows, GRID_W, -1)
    r = np.arange(rows)
    rs = np.clip(r - kr // 2, 0, rows - kr)
    row_idx = rs[:, None] + np.arange(kr)[None, :]
    kb = kg[:, :, row_idx]
    vb = vg[:, :, row_idx]
    cq = np.arange(GRID_W)
    cs = np.clip(cq - NA_COLS // 2, 0, GRID_W - NA_COLS)
    col_ok = (cq[None, :] >= cs[:, None]) & (cq[None, :] < cs[:, None] + NA_COLS)
    roff = row_idx - r[:, None] + (NA_ROWS - 1)
    coff = np.clip(cq[None, :] - cq[:, None] + (NA_COLS - 1), 0, 2 * NA_COLS - 2)
    bias = bias_table[:, roff[:, :, None, None], coff[None, None, :, :]]
    bias = bias.transpose(0, 1, 3, 2, 4).astype(jnp.float32)
    s = jnp.einsum('bhrqd,bhrjkd->bhrqjk', qg, kb).astype(jnp.float32) * scale + bias[None]
    s = jnp.where(col_ok[None, None, None, :, None, :], s, -jnp.inf)
    s = s.reshape(b, h, rows, GRID_W, kr * GRID_W)
    sc = jnp.einsum('bhrqd,bhkd->bhrqk', qg, kc).astype(jnp.float32) * scale
    p = jax.nn.softmax(jnp.concatenate([s, sc], axis=-1), axis=-1).astype(v.dtype)
    pl = p[..., :kr * GRID_W].reshape(b, h, rows, GRID_W, kr, GRID_W)
    pc = p[..., kr * GRID_W:]
    o = jnp.einsum('bhrqjk,bhrjkd->bhrqd', pl, vb) + jnp.einsum('bhrqk,bhkd->bhrqd', pc, vc)
    return o.reshape(b, h, L, -1)

def retention_chunked(q, k, v, log_gamma, s0):
    b, h, L, dk = q.shape
    dv = v.shape[-1]
    C = RET_CHUNK
    n = L // C
    k = k * (dk ** -0.5)
    pos = jnp.arange(C, dtype=jnp.float32)
    lg = log_gamma.astype(jnp.float32)[:, None]
    diff = pos[:, None] - pos[None, :]
    intra = jnp.where(diff >= 0, jnp.exp(lg[:, :, None] * jnp.maximum(diff, 0.0)), 0.0).astype(q.dtype)
    q_dec = jnp.exp(lg * (pos + 1.0)).astype(q.dtype)[None, :, :, None]
    k_dec = jnp.exp(lg * (C - 1.0 - pos)).astype(q.dtype)[None, :, :, None]
    c_dec = jnp.exp(lg * float(C)).astype(q.dtype)[None, :, :, None]

    def chunks(x):
        return x.reshape(b, h, n, C, x.shape[-1]).transpose(2, 0, 1, 3, 4)

    def step(S, inp):
        qi, ki, vi = inp
        inner = jnp.einsum('bhqd,bhkd->bhqk', qi, ki) * intra[None]
        o = jnp.einsum('bhqk,bhkd->bhqd', inner, vi) + jnp.einsum('bhqd,bhde->bhqe', qi * q_dec, S)
        S = S * c_dec + jnp.einsum('bhkd,bhke->bhde', ki * k_dec, vi)
        return S, o

    S, o = lax.scan(step, s0, (chunks(q), chunks(k), chunks(v)))
    return o.transpose(1, 2, 0, 3, 4).reshape(b, h, L, dv), S

def bidir_retention(q, k, v, gates, log_gammas, s0f, s0b, gn_gain):
    of, sf = retention_chunked(q, k, v, log_gammas[0], s0f)
    ob, sb = retention_chunked(jnp.flip(q, 2), jnp.flip(k, 2), jnp.flip(v, 2), log_gammas[1], s0b)
    ob = jnp.flip(ob, 2)
    gf, gb = jnp.split(gates, 2, axis=-1)
    y = jax.nn.silu(gf) * merge_heads(rms_norm(of, gn_gain)) + jax.nn.silu(gb) * merge_heads(rms_norm(ob, gn_gain))
    return y, jnp.stack([sf, sb], axis=1)

def lambda_value(lam_l, lam_init):
    lam_l = lam_l.astype(jnp.float32)
    lq1, lk1, lq2, lk2 = lam_l[0], lam_l[1], lam_l[2], lam_l[3]
    return jnp.exp(jnp.sum(lq1 * lk1)) - jnp.exp(jnp.sum(lq2 * lk2)) + lam_init

def peer(h, wq, subkeys, u_tab, v_tab):
    b, L, D = h.shape
    nb = (b * L) // PEER_TOKEN_BLOCK
    hb = h.reshape(nb, PEER_TOKEN_BLOCK, D)

    def one(xt):
        t = xt.shape[0]
        q = (xt @ wq).reshape(t, PEER_HEADS, 2, PEER_DKEY // 2)
        s1 = jnp.einsum('thd,nd->thn', q[:, :, 0], subkeys[0]).astype(jnp.float32)
        s2 = jnp.einsum('thd,nd->thn', q[:, :, 1], subkeys[1]).astype(jnp.float32)
        v1, i1 = lax.top_k(s1, PEER_TOPK)
        v2, i2 = lax.top_k(s2, PEER_TOPK)
        cand = (v1[..., :, None] + v2[..., None, :]).reshape(t, PEER_HEADS, PEER_TOPK * PEER_TOPK)
        cidx = (i1[..., :, None] * PEER_NKEYS + i2[..., None, :]).reshape(t, PEER_HEADS, PEER_TOPK * PEER_TOPK)
        sc, pos = lax.top_k(cand, PEER_TOPK)
        ids = jnp.take_along_axis(cidx, pos, axis=-1)
        g = jax.nn.softmax(sc, axis=-1).astype(xt.dtype)
        ue = u_tab[ids]
        ve = v_tab[ids]
        a = jax.nn.gelu(jnp.einsum('thkd,td->thk', ue, xt))
        return jnp.einsum('thk,thkd->td', g * a, ve)

    return lax.map(one, hb).reshape(b, L, D)

def modulation(cond, w_mod_l, b_mod_l):
    m = jax.nn.silu(cond) @ w_mod_l + b_mod_l
    return jnp.split(m[:, None, :], 6, axis=-1)

def split_proj(p):
    return jnp.split(p, np.cumsum(IN_WIDTHS)[:-1].tolist(), axis=-1)

def merge_out(mg, ya, yb, yc, wbr_l, wout_l):
    g0, g1, g2 = jnp.split(jax.nn.sigmoid(mg), 3, axis=-1)
    y = g0 * (ya @ wbr_l[0]) + g1 * (yb @ wbr_l[1]) + g2 * (yc @ wbr_l[2])
    return y @ wout_l

def trunk_layer(x, cond, cache, w_mod_l, b_mod_l, norm1_l, w_in_l, lam_l, dgn_l, decay_l, rgn_l, nab_l,
                wbr_l, wout_l, norm2_l, pwq_l, psk_l, pu_l, pv_l, lam_init):
    b = x.shape[0]
    sh1, sc1, g1, sh2, sc2, g2 = modulation(cond, w_mod_l, b_mod_l)
    h = rms_norm(x, norm1_l) * (1 + sc1) + sh1
    qa, ka, va, qb, kb, vb, gb, qc, kc, vc, mg = split_proj(h @ w_in_l)
    qa, ka, va = split_heads(qa, HA), split_heads(ka, HA), split_heads(va, HA)
    qb, kb, vb = split_heads(qb, HB), split_heads(kb, HB), split_heads(vb, HB)
    qc, kc, vc = split_heads(qc, HC), split_heads(kc, HC), split_heads(vc, HC)
    lam = lambda_value(lam_l, lam_init).astype(x.dtype)
    log_gammas = jax.nn.log_sigmoid(decay_l.astype(jnp.float32))
    if cache is None:
        q1, q2 = qa[..., :DA], qa[..., DA:]
        k1, k2 = ka[..., :DA], ka[..., DA:]
        vav = va
        s0f = jnp.zeros((b, HB, DKB, DVB), x.dtype)
        s0b = jnp.zeros((b, HB, DKB, DVB), x.dtype)
        oc = softmax_attn(qc, kc, vc)
    else:
        c_dk, c_dv, c_nk, c_nv, c_st = cache
        q1, q2 = rope_2d(qa[..., :DA]), rope_2d(qa[..., DA:])
        k1 = jnp.concatenate([c_dk[..., :DA], rope_2d(ka[..., :DA])], axis=2)
        k2 = jnp.concatenate([c_dk[..., DA:], rope_2d(ka[..., DA:])], axis=2)
        vav = jnp.concatenate([c_dv, va], axis=2)
        qb, kb = rope_2d(qb), rope_2d(kb)
        s0f, s0b = c_st[:, 0], c_st[:, 1]
        oc = neighbourhood_attn(qc, kc, vc, c_nk, c_nv, nab_l)
    o_diff = softmax_attn(q1, k1, vav) - lam * softmax_attn(q2, k2, vav)
    oa = rms_norm(o_diff, dgn_l) * (1.0 - lam_init)
    ob, s_ret = bidir_retention(qb, kb, vb, gb, log_gammas, s0f, s0b, rgn_l)
    x = x + g1 * merge_out(mg, merge_heads(oa), ob, merge_heads(oc), wbr_l, wout_l)
    h2 = rms_norm(x, norm2_l) * (1 + sc2) + sh2
    x = x + g2 * peer(h2, pwq_l, psk_l, pu_l, pv_l)
    new_ctx = (ka, va, kc, vc, s_ret) if cache is None else None
    return x, new_ctx

def setup_inputs(seed: int = 0) -> dict:
    key = jax.random.key(seed)
    ks = jax.random.split(key, 26)
    f32 = jnp.float32
    nrm = lambda k, s, sc=1.0: jax.random.normal(k, s, f32) * sc
    dec_logit = jnp.log(2.0 ** (5.0 + jnp.arange(HB, dtype=f32)) - 1.0)
    return {
        "x_prompt": nrm(ks[0], (BATCH, SEQ, D_MODEL)),
        "x_sample": nrm(ks[1], (DEC_BATCH, DEC_SEQ, D_MODEL)),
        "c": nrm(ks[2], (DEC_BATCH, D_MODEL)),
        "cache_diff_k": nrm(ks[3], (DEC_BATCH, DEPTH, HA, PAST_LEN, 2 * DA)),
        "cache_diff_v": nrm(ks[4], (DEC_BATCH, DEPTH, HA, PAST_LEN, 2 * DA)),
        "cache_na_k": nrm(ks[5], (DEC_BATCH, DEPTH, HC, PAST_LEN, DC)),
        "cache_na_v": nrm(ks[6], (DEC_BATCH, DEPTH, HC, PAST_LEN, DC)),
        "state_ret": nrm(ks[7], (DEC_BATCH, DEPTH, 2, HB, DKB, DVB)),
        "c_ctx": nrm(ks[8], (D_MODEL,)),
        "w_mod": nrm(ks[9], (DEPTH, D_MODEL, 6 * D_MODEL), 0.5 * D_MODEL ** -0.5),
        "b_mod": nrm(ks[10], (DEPTH, 6 * D_MODEL), 0.01),
        "norm1": 1.0 + nrm(ks[11], (DEPTH, D_MODEL), 0.01),
        "w_in": nrm(ks[12], (DEPTH, D_MODEL, IN_TOTAL), D_MODEL ** -0.5),
        "diff_lambda": nrm(ks[13], (DEPTH, 4, DA), 0.1),
        "diff_gn": 1.0 + nrm(ks[14], (DEPTH, 2 * DA), 0.01),
        "ret_decay": dec_logit + nrm(ks[15], (DEPTH, 2, HB), 0.1),
        "ret_gn": 1.0 + nrm(ks[16], (DEPTH, DVB), 0.01),
        "na_bias": nrm(ks[17], (DEPTH, HC, 2 * NA_ROWS - 1, 2 * NA_COLS - 1), 0.02),
        "w_branch": nrm(ks[18], (DEPTH, N_BRANCH, BRANCH_W, D_MODEL), BRANCH_W ** -0.5),
        "w_out": nrm(ks[19], (DEPTH, D_MODEL, D_MODEL), D_MODEL ** -0.5),
        "norm2": 1.0 + nrm(ks[20], (DEPTH, D_MODEL), 0.01),
        "peer_wq": nrm(ks[21], (DEPTH, D_MODEL, PEER_HEADS * PEER_DKEY), D_MODEL ** -0.5),
        "peer_subkeys": nrm(ks[22], (DEPTH, 2, PEER_NKEYS, PEER_DKEY // 2), (PEER_DKEY // 2) ** -0.5),
        "peer_u": nrm(ks[23], (DEPTH, PEER_N, D_MODEL), D_MODEL ** -0.5),
        "peer_v": nrm(ks[24], (DEPTH, PEER_N, D_MODEL), PEER_HEADS ** -0.5),
        "norm_f": 1.0 + nrm(ks[25], (D_MODEL,), 0.01),
    }

def reference(x_prompt, x_sample, c, cache_diff_k, cache_diff_v, cache_na_k, cache_na_v, state_ret,
              c_ctx, w_mod, b_mod, norm1, w_in, diff_lambda, diff_gn, ret_decay, ret_gn, na_bias,
              w_branch, w_out, norm2, peer_wq, peer_subkeys, peer_u, peer_v, norm_f):
    xp = x_prompt
    cond_ctx = c_ctx[None, :]
    kd, vd, kn, vn, sr = [], [], [], [], []
    for l in range(DEPTH):
        lam_init = 0.8 - 0.6 * math.exp(-0.3 * l)
        xp, ctx = trunk_layer(xp, cond_ctx, None, w_mod[l], b_mod[l], norm1[l], w_in[l], diff_lambda[l],
                              diff_gn[l], ret_decay[l], ret_gn[l], na_bias[l], w_branch[l], w_out[l],
                              norm2[l], peer_wq[l], peer_subkeys[l], peer_u[l], peer_v[l], lam_init)
        kd.append(ctx[0])
        vd.append(ctx[1])
        kn.append(ctx[2])
        vn.append(ctx[3])
        sr.append(ctx[4])
    y_prompt = rms_norm(xp, norm_f)
    new_cache_diff_k = jnp.stack(kd, axis=1)
    new_cache_diff_v = jnp.stack(vd, axis=1)
    new_cache_na_k = jnp.stack(kn, axis=1)
    new_cache_na_v = jnp.stack(vn, axis=1)
    new_state_ret = jnp.stack(sr, axis=1)

    xs = x_sample
    for l in range(DEPTH):
        lam_init = 0.8 - 0.6 * math.exp(-0.3 * l)
        cache = (cache_diff_k[:, l], cache_diff_v[:, l], cache_na_k[:, l], cache_na_v[:, l], state_ret[:, l])
        xs, _ = trunk_layer(xs, c, cache, w_mod[l], b_mod[l], norm1[l], w_in[l], diff_lambda[l],
                            diff_gn[l], ret_decay[l], ret_gn[l], na_bias[l], w_branch[l], w_out[l],
                            norm2[l], peer_wq[l], peer_subkeys[l], peer_u[l], peer_v[l], lam_init)
    y_sample = rms_norm(xs, norm_f)
    return (y_prompt, y_sample, new_cache_diff_k, new_cache_diff_v, new_cache_na_k, new_cache_na_v, new_state_ret)


_drawn_inputs = setup_inputs


def setup_inputs(seed=0):
    import zlib

    import numpy as np

    out = dict(_drawn_inputs(seed))
    spreads = {}
    factors = {'norm1': 4.727,
     'diff_lambda': 5.85,
     'diff_gn': 8.0,
     'ret_gn': 8.0,
     'na_bias': 58.342,
     'norm2': 34.698,
     'norm_f': 31.112,
     'cache_na_k': 8.0,
     'cache_na_v': 8.0}
    for name, (base, spread) in spreads.items():
        noise = np.random.default_rng([zlib.crc32(name.encode()), seed]).standard_normal(out[name].shape)
        drawn = base * np.exp(spread * noise) if base else spread * noise
        out[name] = jnp.asarray(drawn.astype(out[name].dtype))
    for name, factor in factors.items():
        out[name] = (out[name] * factor).astype(out[name].dtype)
    return out
```

```python
from contextlib import ExitStack, contextmanager
import math

import numpy as np

import concourse.bass as bass
from concourse import mybir

F32 = mybir.dt.float32
F32R = mybir.dt.float32r
U32 = mybir.dt.uint32
ALU = mybir.AluOpType
ACT = mybir.ActivationFunctionType
AX_X = mybir.AxisListType.X

P = 128
D = 1024
KD = D // P
DEPTH = 2
NT = 3
TOK = NT * P
LAT = 256
CTX = 128
GRID_W = 64
H = 4
DH = 128
EPS = 1e-6
NEG = -1e30

QA, KA, VA, QB, KB, VB, GB, QC, KC, VC, MG = 0, 512, 1024, 1536, 1792, 2048, 2560, 3584, 4096, 4608, 5120
MIX_W = MG
IN_TOTAL = 8192
NB = 3
BW = 512

PH = 8
NK = 128
TOPK = 16
SLOTS = PH * TOPK

UNIT = 2048
RAW = 4
SPL = 2

C_ID = 0
C_D0 = C_ID + P
C_M0 = C_D0 + 4 * 128
C_IO = C_M0 + 2 * 128
C_NM = C_IO + 256
C_QE = C_NM + 64
C_KE = C_QE + 512
C_COS = C_KE + 2
C_SIN = C_COS + 128
C_SEL = C_SIN + 128
C_LAM = C_SEL + 256
C_ALL = C_LAM + 2 * DEPTH


def constants():
    c = np.zeros((P, C_ALL), np.float32)
    i = np.arange(P)
    c[:, C_ID:C_ID + P] = np.eye(P)
    diff = (i[None, :] - i[:, None]).astype(np.float64)
    c[:, C_D0:C_D0 + 128] = np.maximum(diff, 0)
    c[:, C_D0 + 128:C_D0 + 256] = 128 + diff
    c[:, C_D0 + 256:C_D0 + 384] = np.maximum(-diff, 0)
    c[:, C_D0 + 384:C_D0 + 512] = 128 - diff
    c[:, C_M0:C_M0 + 128] = diff >= 0
    c[:, C_M0 + 128:C_M0 + 256] = diff <= 0
    c[:, C_IO:C_IO + 256] = np.arange(256)[None, :]
    cq, ck = i % GRID_W, np.arange(GRID_W)
    cs = np.clip(cq - 8, 0, GRID_W - 16)[:, None]
    c[:, C_NM:C_NM + 64] = np.where((ck >= cs) & (ck < cs + 16), 0.0, NEG)
    c[:, C_QE:C_QE + 256] = np.arange(256) + 1
    c[:, C_QE + 256:C_QE + 512] = LAT - np.arange(256)
    c[:, C_KE] = CTX - 1 - i
    c[:, C_KE + 1] = i
    half = 32
    freqs = np.float32(10000.0) ** (-np.arange(0, half, 2, dtype=np.float32) / np.float32(half))
    for t in range(2):
        tok = t * P + i
        for a, pos in enumerate((tok // GRID_W, tok % GRID_W)):
            ang = (pos.astype(np.float32)[:, None] * freqs).astype(np.float32).astype(np.float64)
            o = t * 64 + a * 32
            c[:, C_COS + o:C_COS + o + 16] = c[:, C_COS + o + 16:C_COS + o + 32] = np.cos(ang)
            c[:, C_SIN + o:C_SIN + o + 16] = -np.sin(ang)
            c[:, C_SIN + o + 16:C_SIN + o + 32] = np.sin(ang)
    c[[0, 2, 4], C_SEL:C_SEL + 128] = 1.0
    c[[1, 3, 4], C_SEL + 128:C_SEL + 256] = 1.0
    for l in range(DEPTH):
        lam = 0.8 - 0.6 * math.exp(-0.3 * l)
        c[:, C_LAM + 2 * l] = lam
        c[:, C_LAM + 2 * l + 1] = 1.0 - lam
    return c


def sbuf(nc, name, shape, dt=F32):
    return nc.sbuf_tensor(f"{name}_{nc.next_id()}", shape, dt)


def psum(nc, name, shape, dt=F32):
    return nc.psum_tensor(f"{name}_{nc.next_id()}", shape, dt)


class Chain:

    def __init__(self, eng, sem):
        self.eng, self.sem, self.n = eng, sem, 0

    def __call__(self, ins):
        self.n += 1
        ins.then_inc(self.sem, 1)
        self.eng.wait_ge(self.sem, self.n)


@contextmanager
def stage(nc, *names):
    with ExitStack() as ctx:
        sems = [ctx.enter_context(nc.semaphore(f"{n}_{nc.next_id()}")) for n in names]
        yield sems
        for s in sems:
            nc.sync.sem_clear(s)
        nc.all_engine_barrier()


class Buffers:
    pass


def at(l, ap):
    names = " ".join("bcdefg"[:len(ap.shape) - 1])
    first = names.split(" ")[0]
    return ap[bass.ds(l, 1)].rearrange(f"a {names} -> (a {first}) {names[len(first) + 1:]}".strip())


def product(pe, out, ah, al, bh, bl, first, last):
    pe.matmul(out, ah, bh, start=first, stop=False, skip_group_check=True)
    pe.matmul(out, ah, bl, start=False, stop=False, skip_group_check=True)
    return pe.matmul(out, al, bh, start=False, stop=last, skip_group_check=True)



def high_unit(act, b, landed, multiplied, high, n, j):
    act.wait_ge(landed[j % RAW], ((n + j) // RAW + 1) * 16 if isinstance(n, int) else n * (16 // RAW) + 16)
    act.wait_ge(multiplied, n + (j + 1))
    act.activation(b.whi[:, j % SPL, :], b.wraw[:, j % RAW, :], ACT.Copy).then_inc(high, 1)


def low_unit(dve, b, high, split, n, j):
    dve.wait_ge(high, n + (j + 1))
    dve.tensor_tensor(b.wlo[:, j % SPL, :], b.wraw[:, j % RAW, :], b.whi[:, j % SPL, :].bitcast(F32),
                      ALU.subtract).then_inc(split, 1)



def setup(nc, b, a):
    with ExitStack() as ctx:
        cond = ctx.enter_context(sbuf(nc, "cond", [16, P], F32))
        condt = ctx.enter_context(sbuf(nc, "condt", [P, 16], F32))
        ps = ctx.enter_context(psum(nc, "ps_setup", [P, 512], F32))
        with stage(nc, "loaded", "zeroed", "silu_done", "turned", "copied", "hi_done", "lo_done", "biases") as (
                loaded, zeroed, silu_done, turned, copied, hi_done, lo_done, biases), nc.Block() as block:
            @block.sync
            def _(sp):
                sp.dma_start(cond[0:KD, :], a["c_ctx"].rearrange("(k p) -> k p", p=P)).then_inc(loaded, 16)
                sp.dma_start(cond[KD:16, :], a["c"].rearrange("a (k p) -> (a k) p", p=P)).then_inc(loaded, 16)
                sp.dma_start(b.cst[:, :], a["const"]).then_inc(loaded, 16)
                sp.dma_start(b.x[:, 0, :], a["x_prompt"][0]).then_inc(loaded, 16)
                sp.dma_start(b.x[:, 1:3, :], a["x_sample"][0].rearrange("(t p) d -> p t d", p=P)).then_inc(loaded, 16)
                for l in range(DEPTH):
                    for r in range(4):
                        for h in range(H):
                            rows = a["na_pad"][l, h, 7 - r:11 - r, :]
                            src = bass.AP(tensor=rows.tensor, offset=rows.offset + 63,
                                          ap=[[127, 4], [-1, 64], [1, 64]])
                            dst = b.bias[l, 64 * (r % 2):64 * (r % 2) + 64, r // 2, h, :]
                            sp.dma_start(dst.rearrange("p (j n) -> j p n", j=4), src).then_inc(biases, 16)
                sp.wait_ge(loaded, 5 * 16)
                sp.wait_ge(biases, DEPTH * 4 * H * 16)

            @block.scalar
            def _(act):
                act.wait_ge(loaded, 5 * 16)
                act.activation(cond[:, :], cond[:, :], ACT.Silu).then_inc(silu_done, 1)

            @block.tensor
            def _(pe):
                pe.wait_ge(silu_done, 1)
                pe.transpose(ps[:, 0:16], cond[:, :], b.ident[0:16, 0:16]).then_inc(turned, 1)

            @block.vector
            def _(dve):
                dve.memset(b.cnd[:, :, :].bitcast(F32), 0.0).then_inc(zeroed, 1)
                dve.wait_ge(turned, 1)
                dve.tensor_copy(condt[:, :], ps[:, 0:16]).then_inc(copied, 1)
                dve.wait_ge(copied, 1)
                dve.wait_ge(zeroed, 1)
                for j in range(2):
                    dve.tensor_copy(b.cnd[:, :, j], condt[:, KD * j:KD * j + KD]).then_inc(hi_done, 1)
                dve.wait_ge(hi_done, 2)
                for j in range(2):
                    dve.tensor_tensor(b.cnd[:, :, 2 + j], condt[:, KD * j:KD * j + KD],
                                      b.cnd[:, :, j].bitcast(F32), ALU.subtract).then_inc(lo_done, 1)


def modulation(nc, b, a, l):
    N = 6 * D // 512
    w = at(l, a["w_mod"]).rearrange("(q k p) n -> q p k n", p=P, k=4)
    with ExitStack() as ctx:
        rows = ctx.enter_context(sbuf(nc, "mod_rows", [5, 6 * D], F32))
        nrm = ctx.enter_context(sbuf(nc, "norm_rows", [16, P], F32))
        nrmt = ctx.enter_context(sbuf(nc, "norm_cols", [P, 16], F32))
        one = ctx.enter_context(sbuf(nc, "one_plus", [P, 2, KD, 2], F32))
        acc = ctx.enter_context(psum(nc, "mod_acc", [P, 2, 512], F32))
        wide = ctx.enter_context(psum(nc, "mod_wide", [P, 4, 512], F32))
        cols = ctx.enter_context(psum(nc, "mod_cols", [P, 512], F32))
        with stage(nc, *[f"landed{j}" for j in range(RAW)], "small", "high", "split", "multiplied", "stored",
                   "col_done", "wide_done", "wide_copied", "dve_done") as (
                *landed, small, high, split, multiplied, stored, col_done, wide_done, wide_copied, dve_done), \
                nc.Block() as block:
            @block.sync
            def _(sp):
                sp.dma_start(rows[4:5, :], at(l, a["b_mod"]).rearrange("(a n) -> a n", a=1)).then_inc(small, 16)
                sp.dma_start(nrm[0:KD, :], at(l, a["norm1"]).rearrange("(k p) -> k p", p=P)).then_inc(small, 16)
                sp.dma_start(nrm[KD:16, :], at(l, a["norm2"]).rearrange("(k p) -> k p", p=P)).then_inc(small, 16)
                with sp.Fori(0, N // 2) as it:
                    for j in range(4):
                        sp.wait_ge(split, it * 4 + (j + 1))
                        sp.dma_start(b.wraw[:, j, :].rearrange("p (k n) -> p k n", k=4),
                                     w[j % 2][:, :, bass.ds(it * 1024 + (j // 2) * 512, 512)]).then_inc(landed[j], 16)

            @block.scalar
            def _(act):
                with act.Fori(0, N // 2) as it:
                    for j in range(4):
                        high_unit(act, b, landed, multiplied, high, it * 4, j)

            @block.vector
            def _(dve):
                dve.sem_inc(split, RAW)
                dve.sem_inc(stored, 2)

                def store(chunk, half):
                    dve.wait_ge(multiplied, chunk * 2 + (SPL + 2))
                    dve.tensor_scalar(rows[0:4, bass.ds(chunk * 512, 512)], acc[0:4, half, :], 1.0, None,
                                      ALU.mult).then_inc(stored, 1)

                def body(it, last):
                    low_unit(dve, b, high, split, it * 4, 1)
                    low_unit(dve, b, high, split, it * 4, 2)
                    store(it * 2, 0)
                    low_unit(dve, b, high, split, it * 4, 3)
                    if not last:
                        low_unit(dve, b, high, split, it * 4, 4)
                    store(it * 2 + 1, 1)

                low_unit(dve, b, high, split, 0, 0)
                with dve.Fori(0, N // 2 - 1) as it:
                    body(it, False)
                body(N // 2 - 1, True)
                link = Chain(dve, dve_done)
                dve.wait_ge(col_done, 1)
                link(dve.tensor_copy(nrmt[:, :], cols[:, 64:80]))
                mods = cols[:, 0:64].rearrange("p (g k c) -> p g k c", g=4, k=KD)
                link(dve.tensor_copy(b.shift[:, :, :, :], mods[:, 0::2]))
                link(dve.tensor_scalar(one[:, :, :, :], mods[:, 1::2], 1.0, None, ALU.add))
                for s in range(2):
                    link(dve.tensor_tensor(b.scale[:, s], one[:, s],
                                           nrmt[:, KD * s:KD * s + KD].unsqueeze(2).to_broadcast([P, KD, 2]),
                                           ALU.mult))
                for g in range(2):
                    dve.wait_ge(wide_done, g + 1)
                    dve.tensor_copy(b.gate[:, g].rearrange("p c n -> p (c n)"),
                                    wide[:, :, :].rearrange("p a n -> p (a n)")).then_inc(wide_copied, 1)

            @block.tensor
            def _(pe):
                pe.sem_inc(multiplied, SPL)
                with pe.Fori(0, N // 2) as it:
                    for j in range(4):
                        half = j // 2
                        if j % 2 == 0:
                            pe.wait_ge(stored, it * 2 + (half + 1))
                        pe.wait_ge(split, it * 4 + (j + 1 + RAW))
                        for k4 in range(4):
                            k = 4 * (j % 2) + k4
                            c = slice(k4 * 512, k4 * 512 + 512)
                            pe.matmul(acc[:, half, :], b.cnd[:, k, :], b.whi[:, j % SPL, c],
                                      start=(k == 0), stop=False, skip_group_check=True)
                            last = pe.matmul(acc[:, half, :], b.cnd[:, k, :], b.wlo[:, j % SPL, c],
                                             start=False, stop=(k == KD - 1), skip_group_check=True)
                        last.then_inc(multiplied, 1)
                pe.wait_ge(stored, N + 2)
                pe.wait_ge(small, 48)
                sel = b.cst[0:5, C_SEL:C_SEL + 256]
                for g, part in enumerate((0, 1, 3, 4)):
                    for k in range(KD):
                        o = (g * KD + k) * 2
                        pe.matmul(cols[:, o:o + 2], rows[0:5, part * D + k * P:part * D + k * P + P],
                                  sel[:, 0:256:128], start=True, stop=True, skip_group_check=True)
                pe.transpose(cols[:, 64:80], nrm[:, :], b.ident[0:16, 0:16]).then_inc(col_done, 1)
                for g, part in enumerate((2, 5)):
                    if g:
                        pe.wait_ge(wide_copied, g)
                    for c in range(2):
                        for hf in range(2):
                            last = pe.matmul(wide[:, 2 * c + hf, :], sel[:, 128 * c:128 * c + 128],
                                             rows[0:5, part * D + hf * 512:part * D + hf * 512 + 512],
                                             start=True, stop=True, skip_group_check=True)
                    last.then_inc(wide_done, 1)


def norm(nc, b, which):
    with ExitStack() as ctx:
        xn = ctx.enter_context(sbuf(nc, "xn", [P, NT, D], F32))
        h = ctx.enter_context(sbuf(nc, "h", [P, KD, TOK], F32))
        st = ctx.enter_context(sbuf(nc, "norm_stats", [P, 4, NT], F32))
        ps = ctx.enter_context(psum(nc, "ps_norm", [P, NT * 2, 512], F32))
        with stage(nc, "squared", "dve_done", "rooted", "scaled", "turned", "h_done", "hi_done", "lo_done") as (
                squared, dve_done, rooted, scaled, turned, h_done, hi_done, lo_done), nc.Block() as block:
            @block.scalar
            def _(act):
                for t in range(NT):
                    act.activation(xn[:, t, :], b.x[:, t, :], ACT.Square,
                                   accum_out=st[:, 0, t:t + 1]).then_inc(squared, 1)
                act.wait_ge(dve_done, 1)
                act.activation(st[:, 2, :], st[:, 1, :], ACT.Sqrt).then_inc(rooted, 1)
                for t in range(NT):
                    act.wait_ge(h_done, t + 1)
                    act.activation(b.hhi[:, :, t * P:t * P + P], h[:, :, t * P:t * P + P],
                                   ACT.Copy).then_inc(hi_done, 1)

            @block.vector
            def _(dve):
                link = Chain(dve, dve_done)
                dve.wait_ge(squared, NT)
                link(dve.tensor_scalar(st[:, 1, :], st[:, 0, :], 1.0 / D, EPS, ALU.mult, ALU.add))
                dve.wait_ge(rooted, 1)
                link(dve.reciprocal(st[:, 3, :], st[:, 2, :]))
                for t in range(NT):
                    dve.tensor_scalar(xn[:, t, :], b.x[:, t, :], st[:, 3, t:t + 1], None,
                                      ALU.mult).then_inc(scaled, 1)
                for t in range(NT):
                    dve.wait_ge(turned, t + 1)
                    for k in range(KD):
                        c = min(t, 1)
                        last = dve.tensor_scalar(h[:, k, t * P:t * P + P],
                                                 ps[:, 2 * t + k // 4, (k % 4) * P:(k % 4) * P + P],
                                                 b.scale[:, which, k, c:c + 1], b.shift[:, which, k, c:c + 1],
                                                 ALU.mult, ALU.add)
                    last.then_inc(h_done, 1)
                for t in range(NT):
                    dve.wait_ge(hi_done, t + 1)
                    dve.tensor_tensor(b.hlo[:, :, t * P:t * P + P], h[:, :, t * P:t * P + P],
                                      b.hhi[:, :, t * P:t * P + P].bitcast(F32), ALU.subtract).then_inc(lo_done, 1)

            @block.tensor
            def _(pe):
                for t in range(NT):
                    pe.wait_ge(scaled, t + 1)
                    for k in range(KD):
                        last = pe.transpose(ps[:, 2 * t + k // 4, (k % 4) * P:(k % 4) * P + P],
                                            xn[:, t, k * P:k * P + P], b.ident)
                    last.then_inc(turned, 1)


def project(nc, b, a, l):
    N = MIX_W // 512
    w = at(l, a["w_in"]).rearrange("(q k p) n -> q p k n", p=P, k=4)
    with ExitStack() as ctx:
        acc = ctx.enter_context(psum(nc, "proj_acc", [P, 2 * NT, 512], F32))
        with stage(nc, *[f"landed{j}" for j in range(RAW)], "high", "split", "multiplied", "stored") as (
                *landed, high, split, multiplied, stored), nc.Block() as block:
            @block.sync
            def _(sp):
                with sp.Fori(0, N // 2) as it:
                    for j in range(4):
                        sp.wait_ge(split, it * 4 + (j + 1))
                        sp.dma_start(b.wraw[:, j, :].rearrange("p (k n) -> p k n", k=4),
                                     w[j % 2][:, :, bass.ds(it * 1024 + (j // 2) * 512, 512)]).then_inc(landed[j], 16)

            @block.scalar
            def _(act):
                with act.Fori(0, N // 2) as it:
                    for j in range(4):
                        high_unit(act, b, landed, multiplied, high, it * 4, j)

            @block.vector
            def _(dve):
                dve.sem_inc(split, RAW)
                dve.sem_inc(stored, 2)

                def store(chunk, half):
                    dve.wait_ge(multiplied, chunk * 2 + (SPL + 2))
                    dve.tensor_scalar(b.proj[:, :, bass.ds(chunk * 512, 512)],
                                      acc[:, NT * half:NT * half + NT, :], 1.0, None, ALU.mult).then_inc(stored, 1)

                def body(it, last):
                    low_unit(dve, b, high, split, it * 4, 1)
                    low_unit(dve, b, high, split, it * 4, 2)
                    store(it * 2, 0)
                    low_unit(dve, b, high, split, it * 4, 3)
                    if not last:
                        low_unit(dve, b, high, split, it * 4, 4)
                    store(it * 2 + 1, 1)

                low_unit(dve, b, high, split, 0, 0)
                with dve.Fori(0, N // 2 - 1) as it:
                    body(it, False)
                body(N // 2 - 1, True)

            @block.tensor
            def _(pe):
                pe.sem_inc(multiplied, SPL)
                with pe.Fori(0, N // 2) as it:
                    for j in range(4):
                        half = j // 2
                        if j % 2 == 0:
                            pe.wait_ge(stored, it * 2 + (half + 1))
                        pe.wait_ge(split, it * 4 + (j + 1 + RAW))
                        for k4 in range(4):
                            k = 4 * (j % 2) + k4
                            c = slice(k4 * 512, k4 * 512 + 512)
                            for t in range(NT):
                                r = slice(t * P, t * P + P)
                                last = product(pe, acc[:, NT * half + t, :], b.hhi[:, k, r], b.hlo[:, k, r],
                                               b.whi[:, j % SPL, c], b.wlo[:, j % SPL, c], k == 0, k == KD - 1)
                        last.then_inc(multiplied, 1)


def rotary(nc, b):
    with ExitStack() as ctx:
        swap = ctx.enter_context(sbuf(nc, "rope_swap", [P, 2, 1536], F32))
        with stage(nc, "swapped", "scaled", "added") as (swapped, scaled, added), nc.Block() as block:
            parts = [(t, c, n, o) for t in range(2) for c, n, o in ((QA, 1024, 0), (QB, 512, 1024))]

            @block.vector
            def _(dve):
                for t, c, n, o in parts:
                    x = b.proj[:, 1 + t, c:c + n].rearrange("p (g a j d) -> p g a j d", a=2, j=2, d=16)
                    s = swap[:, t, o:o + n].rearrange("p (g a j d) -> p g a j d", a=2, j=2, d=16)
                    sin = b.cst[:, C_SIN + 64 * t:C_SIN + 64 * t + 64].rearrange("p (a j d) -> p a j d", a=2, j=2)
                    for j in range(2):
                        dve.tensor_tensor(s[:, :, :, j, :], x[:, :, :, 1 - j, :],
                                          sin[:, :, j, :].unsqueeze(1).to_broadcast([P, n // 64, 2, 16]),
                                          ALU.mult).then_inc(swapped, 1)
                dve.wait_ge(swapped, 8)
                for t, c, n, o in parts:
                    x = b.proj[:, 1 + t, c:c + n].rearrange("p (g d) -> p g d", d=64)
                    cos = b.cst[:, C_COS + 64 * t:C_COS + 64 * t + 64]
                    dve.tensor_tensor(x, x, cos.unsqueeze(1).to_broadcast([P, n // 64, 64]),
                                      ALU.mult).then_inc(scaled, 1)
                dve.wait_ge(scaled, 4)
                for t, c, n, o in parts:
                    x = b.proj[:, 1 + t, c:c + n]
                    dve.tensor_tensor(x, x, swap[:, t, o:o + n], ALU.add).then_inc(added, 1)

            @block.sync
            def _(sp):
                sp.wait_ge(added, 4)


def turn_heads(pe, b, tp, turns, turned, turns_copied):
    for n in range(len(turns) // 4):
        if n >= 2:
            pe.wait_ge(turns_copied, n - 1)
        for i in range(4):
            last = pe.transpose(tp[:, n % 2, i * P:i * P + P], turns[4 * n + i], b.ident)
        last.then_inc(turned, 1)


def copy_turns(act, tp, heads, count, turned, turns_copied):
    for n in range(count // 4):
        act.wait_ge(turned, n + 1)
        act.activation(heads[:, 4 * n:4 * n + 4, :].rearrange("p a t -> p (a t)"), tp[:, n % 2, :],
                       ACT.Copy).then_inc(turns_copied, 1)


def attention(nc, b, a, l, diff):
    q0, k0, v0 = (QA, KA, VA) if diff else (QC, KC, VC)
    ck, cv = ("cache_diff_k", "cache_diff_v") if diff else ("cache_na_k", "cache_na_v")
    ok, ov = ("o_diff_k", "o_diff_v") if diff else ("o_na_k", "o_na_v")
    S = 2 if diff else 1
    DQ = DH // S
    SC = float(DQ) ** -0.5
    units = [(t, h) for t in range(NT) for h in range(H)]
    U = len(units)
    with ExitStack() as ctx:
        sb = lambda n, s: ctx.enter_context(sbuf(nc, n, s, F32))
        ps = lambda n, s: ctx.enter_context(psum(nc, n, s, F32))
        heads = sb("heads", [P, 7 * H, P])
        qt = heads[:, 0:NT * H, :].rearrange("p (h t) n -> p h t n", h=H)
        kt = heads[:, NT * H:7 * H, :].rearrange("p (h s) n -> p h (s n)", h=H)
        kc = sb("cache_k", [P, H, DH])
        vc = sb("cache_v", [P, H, DH])
        pr = sb("probs", [P, 2, S, 384])
        pt = sb("probs_t", [P, 2, 384])
        o = sb("heads_out", [P, U, DH])
        st = sb("softmax_stats", [P, 6, U, 2])
        mx, nm, sm, rc, r2 = (st[:, i] for i in range(5))
        if diff:
            lq = sb("lambda_in", [P, 4, 64])
            lt = sb("lambda_work", [P, 2, 64])
            lw = sb("lambda_vals", [P, 8])
            gn = sb("diff_gain", [P, DH])
            sq = sb("squares", [P, U, DH])
            hs = sb("head_stats", [P, 4, U])
        else:
            bias = sb("na_bias", [P, 2, H, LAT])
            sc = sb("scores", [P, 2, 384])
        tp = ps("ps_turn", [P, 2, 512])
        s = ps("ps_scores", [P, 2, S, 512])
        p2 = ps("ps_probs", [P, 512])
        po = ps("ps_out", [P, 512])

        def keys(t):
            return (0, 1) if t == 0 else (1, 3)

        with stage(nc, "loaded", "written", "turned", "turns_copied", "scored", "dve_done", "shifted", "expd",
                   "weighed", "p_turned", "p_copied", "o_done", "o_copied", "lam_sum", "lam_exp", "rooted",
                   "biased") as (
                loaded, written, turned, turns_copied, scored, dve_done, shifted, expd, weighed, p_turned,
                p_copied, o_done, o_copied, lam_sum, lam_exp, rooted, biased), nc.Block() as block:
            LOADS = 4 if diff else 3

            @block.sync
            def _(sp):
                sp.dma_start(kc[:, :, :], at(l, a[ck][0]).rearrange("h s d -> s h d")).then_inc(loaded, 16)
                sp.dma_start(vc[:, :, :], at(l, a[cv][0]).rearrange("h s d -> s h d")).then_inc(loaded, 16)
                if diff:
                    sp.dma_start(lq[:, :, :], at(l, a["diff_lambda"]).partition_broadcast(P)).then_inc(loaded, 16)
                    sp.dma_start(gn[:, :], at(l, a["diff_gn"]).partition_broadcast(P)).then_inc(loaded, 16)
                else:
                    sp.dma_start(bias[:, :, :, :], at(l, b.bias)).then_inc(loaded, 16)
                for out, col in ((ok, k0), (ov, v0)):
                    sp.dma_start(at(l, a[out][0]).rearrange("h s d -> s h d"),
                                 b.proj[:, 0, col:col + 512].rearrange("p (h d) -> p h d", h=H)).then_inc(written, 16)
                sp.wait_ge(written, 32)

            @block.scalar
            def _(act):
                copy_turns(act, tp, heads, 7 * H, turned, turns_copied)
                if diff:
                    act.wait_ge(lam_sum, 1)
                    act.activation(lw[:, 2:4], lw[:, 0:2], ACT.Exp).then_inc(lam_exp, 1)

                def exps(u):
                    t, h = units[u]
                    n = keys(t)[1] * P
                    act.wait_ge(shifted, u + 1)
                    if u >= 2:
                        act.wait_ge(p_turned, u - 1)
                    for i in range(S):
                        if diff:
                            act.activation(pr[:, u % 2, i, 0:n], s[:, u % 2, i, 0:n], ACT.Exp,
                                           bias=nm[:, u, i:i + 1], scale=SC,
                                           accum_out=sm[:, u, i:i + 1]).then_inc(expd, 1)
                        else:
                            act.activation(pr[:, u % 2, 0, 0:n], sc[:, u % 2, 0:n], ACT.Exp,
                                           bias=nm[:, u, 0:1], accum_out=sm[:, u, 0:1]).then_inc(expd, 1)

                def probs_out(u):
                    n = keys(units[u][0])[1] * P
                    act.wait_ge(p_turned, u + 1)
                    if u >= 2:
                        act.wait_ge(o_done, u - 1)
                    act.activation(pt[:, u % 2, 0:n], p2[:, 0:n], ACT.Copy).then_inc(p_copied, 1)

                for u in range(U + 1):
                    if u < U:
                        exps(u)
                    if u >= 1:
                        probs_out(u - 1)
                if diff:
                    act.wait_ge(rooted, 1)
                    act.activation(hs[:, 2, :], hs[:, 1, :], ACT.Sqrt).then_inc(rooted, 1)

            @block.vector
            def _(dve):
                link = Chain(dve, dve_done)
                dve.wait_ge(loaded, 16 * LOADS)
                if diff:
                    link(dve.tensor_copy(lw[:, 4:6], b.cst[:, bass.ds(C_LAM + 2 * l, 2)]))
                    link(dve.tensor_tensor(lt[:, :, :], lq[:, 0::2, :], lq[:, 1::2, :], ALU.mult))
                    dve.tensor_reduce(lw[:, 0:2], lt[:, :, :], AX_X, ALU.add).then_inc(lam_sum, 1)
                    dve.wait_ge(lam_exp, 1)
                    link(dve.tensor_tensor(lw[:, 6:7], lw[:, 3:4], lw[:, 2:3], ALU.subtract))
                    link(dve.tensor_tensor(lw[:, 7:8], lw[:, 6:7], lw[:, 4:5], ALU.subtract))
                    link(dve.tensor_scalar(gn[:, :], gn[:, :], lw[:, 5:6], None, ALU.mult))
                else:
                    link(dve.tensor_tensor(
                        bias[:, :, :, :].rearrange("p a h (j n) -> p (a h j) n", j=4),
                        bias[:, :, :, :].rearrange("p a h (j n) -> p (a h j) n", j=4),
                        b.cst[:, C_NM:C_NM + 64].unsqueeze(1).to_broadcast([P, 32, 64]), ALU.add))

                def maxima(u):
                    t, h = units[u]
                    n = keys(t)[1] * P
                    dve.wait_ge(scored, u + 1)
                    if diff:
                        link(dve.tensor_reduce(mx[:, u, :], s[:, u % 2, :, 0:n], AX_X, ALU.max))
                        dve.tensor_scalar(nm[:, u, :], mx[:, u, :], -SC, None, ALU.mult).then_inc(shifted, 1)
                        return
                    if u >= 2:
                        dve.wait_ge(expd, u - 1)
                    if t == 0:
                        link(dve.tensor_scalar(sc[:, u % 2, 0:n], s[:, u % 2, 0, 0:n], SC, None, ALU.mult))
                    else:
                        dve.tensor_scalar(sc[:, u % 2, 0:P], s[:, u % 2, 0, 0:P], SC, None,
                                          ALU.mult).then_inc(biased, 1)
                        link(dve.scalar_tensor_tensor(sc[:, u % 2, P:n], s[:, u % 2, 0, P:n], SC,
                                                      bias[:, t - 1, h, :], ALU.mult, ALU.add))
                        dve.wait_ge(biased, u + 1 - H)
                    link(dve.tensor_reduce(mx[:, u, 0:1], sc[:, u % 2, 0:n], AX_X, ALU.max))
                    dve.tensor_scalar(nm[:, u, 0:1], mx[:, u, 0:1], -1.0, None, ALU.mult).then_inc(shifted, 1)

                def weigh(u):
                    n = keys(units[u][0])[1] * P
                    dve.wait_ge(expd, S * (u + 1))
                    link(dve.reciprocal(rc[:, u, 0:S], sm[:, u, 0:S]))
                    if diff:
                        link(dve.tensor_scalar(r2[:, u, 1:2], rc[:, u, 1:2], lw[:, 7:8], None, ALU.mult))
                        link(dve.tensor_scalar(pr[:, u % 2, 0, 0:n], pr[:, u % 2, 0, 0:n], rc[:, u, 0:1], None,
                                               ALU.mult))
                        dve.scalar_tensor_tensor(pr[:, u % 2, 0, 0:n], pr[:, u % 2, 1, 0:n], r2[:, u, 1:2],
                                                 pr[:, u % 2, 0, 0:n], ALU.mult, ALU.add).then_inc(weighed, 1)

                def out(u):
                    t, h = units[u]
                    dve.wait_ge(o_done, u + 1)
                    if diff:
                        dve.tensor_copy(o[:, u, :], po[:, 0:DH]).then_inc(o_copied, 1)
                    else:
                        dve.tensor_scalar(b.y[:, t, 2, h * DH:h * DH + DH], po[:, 0:DH], rc[:, u, 0:1], None,
                                          ALU.mult).then_inc(o_copied, 1)

                maxima(0)
                for u in range(U + 2):
                    if u + 1 < U:
                        maxima(u + 1)
                    if u < U:
                        weigh(u)
                    if u >= 2:
                        out(u - 2)
                if diff:
                    dve.wait_ge(o_copied, U)
                    link(dve.tensor_tensor(sq[:, :, :], o[:, :, :], o[:, :, :], ALU.mult))
                    link(dve.tensor_reduce(hs[:, 0, :], sq[:, :, :], AX_X, ALU.add))
                    dve.tensor_scalar(hs[:, 1, :], hs[:, 0, :], 1.0 / DH, EPS, ALU.mult, ALU.add).then_inc(rooted, 1)
                    dve.wait_ge(rooted, 2)
                    link(dve.reciprocal(hs[:, 3, :], hs[:, 2, :]))
                    link(dve.tensor_tensor(sq[:, :, :], o[:, :, :],
                                           hs[:, 3, :].unsqueeze(2).to_broadcast([P, U, DH]), ALU.mult))
                    link(dve.tensor_tensor(b.y[:, :, 0, :].rearrange("p t (h d) -> p t h d", h=H),
                                           sq[:, :, :].rearrange("p (t h) d -> p t h d", h=H),
                                           gn[:, :].unsqueeze(1).unsqueeze(1).to_broadcast([P, NT, H, DH]), ALU.mult))

            @block.tensor
            def _(pe):
                q = [b.proj[:, t, q0 + h * DH:q0 + h * DH + DH] for h in range(H) for t in range(NT)]
                k = []
                for h in range(H):
                    own = [b.proj[:, t, k0 + h * DH:k0 + h * DH + DH] for t in range(NT)]
                    k += [own[0], kc[:, h, :], own[1], own[2]]
                pe.wait_ge(loaded, 16 * LOADS)
                turn_heads(pe, b, tp, q + k, turned, turns_copied)
                pe.wait_ge(turns_copied, 7)

                def scores(u):
                    t, h = units[u]
                    f, n = keys(t)
                    if u >= 2:
                        if diff:
                            pe.wait_ge(expd, S * (u - 1))
                        else:
                            pe.wait_ge(shifted, u - 1)
                    for i in range(S):
                        r = slice(DQ * i, DQ * i + DQ)
                        last = pe.matmul(s[:, u % 2, i, 0:n * P], qt[r, h, t, :], kt[r, h, f * P:(f + n) * P],
                                         start=True, stop=True, skip_group_check=True)
                    last.then_inc(scored, 1)

                def turn_probs(u):
                    n = keys(units[u][0])[1]
                    if diff:
                        pe.wait_ge(weighed, u + 1)
                    else:
                        pe.wait_ge(expd, u + 1)
                    if u >= 1:
                        pe.wait_ge(p_copied, u)
                    for i in range(n):
                        last = pe.transpose(p2[:, i * P:i * P + P], pr[:, u % 2, 0, i * P:i * P + P], b.ident)
                    last.then_inc(p_turned, 1)

                def values(u):
                    t, h = units[u]
                    v = [b.proj[:, i, v0 + h * DH:v0 + h * DH + DH] for i in range(NT)]
                    v = [v[0]] if t == 0 else [vc[:, h, :], v[1], v[2]]
                    pe.wait_ge(p_copied, u + 1)
                    if u >= 1:
                        pe.wait_ge(o_copied, u)
                    for i, vi in enumerate(v):
                        last = pe.matmul(po[:, 0:DH], pt[:, u % 2, i * P:i * P + P], vi,
                                         start=(i == 0), stop=(i == len(v) - 1), skip_group_check=True)
                    last.then_inc(o_done, 1)

                scores(0)
                for u in range(U + 1):
                    if u + 1 < U:
                        scores(u + 1)
                    if u < U:
                        turn_probs(u)
                    if u >= 1:
                        values(u - 1)


def retention(nc, b, a, l):
    PR = H // 2
    with ExitStack() as ctx:
        sb = lambda n, s: ctx.enter_context(sbuf(nc, n, s, F32))
        ps = lambda n, s: ctx.enter_context(psum(nc, n, s, F32))
        heads = sb("ret_heads", [P, 12, P])
        dec = sb("ret_decay", [P, 8])
        lg = sb("log_gamma", [P, 8])
        lgp = sb("log_gamma_pairs", [P, 2, PR])
        lw = sb("log_work", [P, 6, 8])
        gn = sb("ret_gain", [P, DH])
        s0 = sb("ret_state", [P, 2, PR, DH])
        dm = sb("decay_mats", [P, 2, H, 2, P])
        qd = sb("q_decay", [P, 2, PR, LAT])
        ke = sb("k_decay", [P, 2, H])
        kd = sb("k_decayed", [P, H, 2, 64])
        sa = sb("decayed_scores", [P, 1, 2, 4, P])
        og = sb("ret_out", [P, 2, NT, H, DH])
        sq = sb("ret_squares", [P, NT, H, DH])
        hs = sb("ret_stats", [P, 4, 2 * NT * H])
        so = sb("state_out", [64, 2, H, DH])
        tp = ps("ps_turn", [P, 2, 512])
        s = ps("ps_scores", [P, 2, 512])
        po = ps("ps_out", [P, 2, 512])
        pst = ps("ps_state", [64, 2, 512])
        with stage(nc, "loaded", "written", "turned", "turns_copied", "scored", "dve_done", "act_done", "mats",
                   "masked", "s_decayed", "o_done", "o_copied", "k_scaled", "states", "s_out", "edges", "q_ready",
                   "squared", "act_ask") as (
                loaded, written, turned, turns_copied, scored, dve_done, act_done, mats, masked, s_decayed, o_done,
                o_copied, k_scaled, states, s_out, edges, q_ready, squared, act_ask), nc.Block() as block:
            @block.sync
            def _(sp):
                sp.dma_start(dec[:, :], at(l, a["ret_decay"]).rearrange("d h -> (d h)").partition_broadcast(P))\
                    .then_inc(loaded, 16)
                sp.dma_start(gn[:, :], at(l, a["ret_gn"]).partition_broadcast(P)).then_inc(loaded, 16)
                for d in range(2):
                    sp.dma_start(s0[:, d, :, :], at(l, a["state_ret"][0])[d].rearrange("(r h) k v -> (h k) r v", h=2))\
                        .then_inc(loaded, 16)
                sp.wait_ge(s_out, 2)
                for d in range(2):
                    sp.dma_start(at(l, a["o_state"][0])[d].rearrange("h k v -> k h v"), so[:, d, :, :])\
                        .then_inc(written, 16)
                sp.wait_ge(written, 32)

            @block.scalar
            def _(act):
                act.wait_ge(loaded, 64)
                act.activation(lw[:, 0, :], dec[:, :], ACT.Abs).then_inc(act_done, 1)
                act.wait_ge(act_done, 1)
                act.activation(lw[:, 1, :], lw[:, 0, :], ACT.Exp, scale=-1.0).then_inc(act_done, 1)
                copy_turns(act, tp, heads, 12, turned, turns_copied)
                act.wait_ge(act_ask, 1)
                for d in range(2):
                    for h in range(H):
                        i = d * H + h
                        act.activation(dm[:, d, h, :, :].rearrange("p a t -> p (a t)"),
                                       b.cst[:, C_D0 + 256 * d:C_D0 + 256 * d + 256], ACT.Exp,
                                       scale=lg[:, i:i + 1]).then_inc(mats, 1)
                        act.activation(ke[:, d, h:h + 1], b.cst[:, C_KE + d:C_KE + d + 1], ACT.Exp,
                                       scale=lg[:, i:i + 1]).then_inc(mats, 1)
                for d in range(2):
                    for r in range(PR):
                        act.activation(qd[:, d, r, :], b.cst[:, C_QE + 256 * d:C_QE + 256 * d + 256], ACT.Exp,
                                       scale=lgp[:, d, r:r + 1]).then_inc(edges, 1)
                act.wait_ge(act_ask, 2)
                act.activation(hs[:, 2, :], hs[:, 1, :], ACT.Sqrt).then_inc(act_done, 1)
                act.activation(b.proj[:, :, GB:GB + 1024], b.proj[:, :, GB:GB + 1024], ACT.Silu)\
                    .then_inc(act_done, 1)

            @block.vector
            def _(dve):
                link = Chain(dve, dve_done)
                dve.wait_ge(act_done, 2)
                e, z, z2, q, w = (lw[:, i, :] for i in (1, 2, 3, 4, 5))
                link(dve.tensor_scalar(z, e, 2.0, None, ALU.add))
                link(dve.reciprocal(z2, z))
                link(dve.tensor_tensor(z, e, z2, ALU.mult))
                link(dve.tensor_tensor(z2, z, z, ALU.mult))
                link(dve.tensor_scalar(q, z2, 2.0 / 17, 2.0 / 15, ALU.mult, ALU.add))
                for n in (13, 11, 9, 7, 5, 3, 1):
                    link(dve.tensor_tensor(w, q, z2, ALU.mult))
                    link(dve.tensor_scalar(q, w, 2.0 / n, None, ALU.add))
                link(dve.tensor_tensor(w, q, z, ALU.mult))
                link(dve.tensor_scalar(q, dec[:, :], 0.0, None, ALU.min))
                link(dve.tensor_tensor(lg[:, :], q, w, ALU.subtract))
                pairs = lg[:, :].rearrange("p (d r h) -> p d r h", d=2, h=2)
                link(dve.tensor_copy(lgp[0:64], pairs[0:64, :, :, 0]))
                dve.tensor_copy(lgp[64:128], pairs[64:128, :, :, 1]).then_inc(act_ask, 1)
                dve.wait_ge(mats, 16)
                for d in range(2):
                    m = b.cst[:, C_M0 + 128 * d:C_M0 + 128 * d + 128]
                    dve.scalar_tensor_tensor(dm[:, d, :, 0, :], dm[:, d, :, 0, :], 0.125,
                                             m.unsqueeze(1).to_broadcast([P, H, P]), ALU.mult, ALU.mult)\
                        .then_inc(masked, 1)
                    dve.tensor_scalar(dm[:, d, :, 1, :], dm[:, d, :, 1, :], 0.125, None, ALU.mult).then_inc(masked, 1)
                link(dve.tensor_scalar(ke[:, :, :], ke[:, :, :], 0.125, None, ALU.mult))
                for d in range(2):
                    for h in range(H):
                        dve.tensor_scalar(kd[:, h, d, :], b.proj[:, 0, KB + 64 * h:KB + 64 * h + 64],
                                          ke[:, d, h:h + 1], None, ALU.mult).then_inc(k_scaled, 1)
                dve.wait_ge(edges, 4)
                dve.wait_ge(turns_copied, 3)
                qt = heads[:, 0:6, :].rearrange("p (r t) n -> p r (t n)", r=PR)
                for d in range(2):
                    dve.tensor_tensor(qd[:, d], qd[:, d], qt[:, :, P:3 * P], ALU.mult).then_inc(q_ready, 1)
                dve.wait_ge(masked, 4)
                for h in range(H):
                    dve.wait_ge(scored, h + 1)
                    if h >= 1:
                        dve.wait_ge(o_done, h)
                    sf, sbk = sa[:, 0, 0], sa[:, 0, 1]
                    f, k = dm[:, 0, h], dm[:, 1, h]
                    dve.tensor_tensor(sf[:, 0, :], s[:, 0, 0:128], f[:, 0, :], ALU.mult).then_inc(s_decayed, 1)
                    dve.tensor_tensor(sf[:, 1:3, :], s[:, 0, 128:384].rearrange("p (a t) -> p a t", a=2), f,
                                      ALU.mult).then_inc(s_decayed, 1)
                    dve.tensor_tensor(sf[:, 3, :], s[:, 1, 128:256], f[:, 0, :], ALU.mult).then_inc(s_decayed, 1)
                    dve.tensor_tensor(sbk[:, 0:2, :], s[:, 0, 0:256].rearrange("p (a t) -> p a t", a=2),
                                      k[:, 0, :].unsqueeze(1).to_broadcast([P, 2, P]), ALU.mult)\
                        .then_inc(s_decayed, 1)
                    dve.tensor_tensor(sbk[:, 2, :], s[:, 1, 0:128], k[:, 1, :], ALU.mult).then_inc(s_decayed, 1)
                    dve.tensor_tensor(sbk[:, 3, :], s[:, 1, 128:256], k[:, 0, :], ALU.mult).then_inc(s_decayed, 1)
                    dve.wait_ge(o_done, h + 1)
                    dve.tensor_copy(og[:, :, :, h, :],
                                    po[:, :, 0:NT * P].rearrange("p d (t n) -> p d t n", t=NT)).then_inc(o_copied, 1)
                dve.wait_ge(states, 1)
                dve.wait_ge(o_copied, H)
                for d in range(2):
                    dve.tensor_copy(so[:, d, :, :], pst[:, d, :].rearrange("p (h v) -> p h v", h=H)).then_inc(s_out, 1)
                HN = NT * H
                for d in range(2):
                    link(dve.tensor_tensor(sq[:, :, :, :].rearrange("p t h v -> p (t h v)"),
                                           og[:, d].rearrange("p t h v -> p (t h v)"),
                                           og[:, d].rearrange("p t h v -> p (t h v)"), ALU.mult))
                    link(dve.tensor_reduce(hs[:, 0, HN * d:HN * d + HN],
                                           sq[:, :, :, :].rearrange("p t h v -> p (t h) v"), AX_X, ALU.add))
                dve.tensor_scalar(hs[:, 1, :], hs[:, 0, :], 1.0 / DH, EPS, ALU.mult, ALU.add).then_inc(act_ask, 1)
                dve.wait_ge(act_done, 4)
                link(dve.reciprocal(hs[:, 3, :], hs[:, 2, :]))
                flat = og[:, :, :, :, :].rearrange("p d t h v -> p (d t h) v")
                link(dve.tensor_tensor(flat, flat, hs[:, 3, :].unsqueeze(2).to_broadcast([P, 2 * HN, DH]), ALU.mult))
                link(dve.tensor_tensor(flat, flat, gn[:, :].unsqueeze(1).to_broadcast([P, 2 * HN, DH]), ALU.mult))
                for d in range(2):
                    v = og[:, d].rearrange("p t h v -> p t (h v)")
                    link(dve.tensor_tensor(v, v, b.proj[:, :, GB + 512 * d:GB + 512 * d + 512], ALU.mult))
                link(dve.tensor_tensor(b.y[:, :, 1, :], og[:, 0].rearrange("p t h v -> p t (h v)"),
                                       og[:, 1].rearrange("p t h v -> p t (h v)"), ALU.add))

            @block.tensor
            def _(pe):
                turns = [b.proj[:, t, c + r * P:c + r * P + P] for c in (QB, KB) for r in range(PR) for t in range(NT)]
                turn_heads(pe, b, tp, turns, turned, turns_copied)
                pe.wait_ge(turns_copied, 3)
                qt = heads[:, 0:6, :].rearrange("p (r t) n -> p r (t n)", r=PR)
                kt = heads[:, 6:12, :].rearrange("p (r t) n -> p r (t n)", r=PR)
                for h in range(H):
                    r, rows = h // 2, slice(64 * (h % 2), 64 * (h % 2) + 64)
                    v = [b.proj[:, t, VB + h * DH:VB + h * DH + DH] for t in range(NT)]
                    if h >= 1:
                        pe.wait_ge(s_decayed, 6 * h)
                    pe.matmul(s[:, 0, 0:P], kt[rows, r, 0:P], qt[rows, r, 0:P], start=True, stop=True,
                              skip_group_check=True)
                    pe.matmul(s[:, 0, P:3 * P], kt[rows, r, P:2 * P], qt[rows, r, P:3 * P], start=True, stop=True,
                              skip_group_check=True)
                    pe.matmul(s[:, 1, 0:2 * P], kt[rows, r, 2 * P:3 * P], qt[rows, r, P:3 * P], start=True,
                              stop=True, skip_group_check=True).then_inc(scored, 1)
                    pe.wait_ge(s_decayed, 6 * h + 6)
                    pe.wait_ge(q_ready, 2)
                    if h >= 1:
                        pe.wait_ge(o_copied, h)
                    terms = {(0, 0): [(0, 0)], (0, 1): [(1, 1)], (0, 2): [(2, 1), (3, 2)],
                             (1, 0): [(0, 0)], (1, 1): [(1, 1), (2, 2)], (1, 2): [(3, 2)]}
                    for (d, t), blocks in terms.items():
                        out = po[:, d, t * P:t * P + P]
                        for i, (blk, vt) in enumerate(blocks):
                            last = pe.matmul(out, sa[:, 0, d, blk, :], v[vt], start=(i == 0),
                                             stop=(t == 0 and i == len(blocks) - 1), skip_group_check=True)
                        if t:
                            last = pe.matmul(out, qd[rows, d, r, (t - 1) * P:t * P], s0[rows, d, r, :], start=False,
                                             stop=True, skip_group_check=True)
                    last.then_inc(o_done, 1)
                pe.wait_ge(k_scaled, 8)
                for d in range(2):
                    for h in range(H):
                        last = pe.matmul(pst[:, d, h * DH:h * DH + DH], kd[:, h, d, :],
                                         b.proj[:, 0, VB + h * DH:VB + h * DH + DH], start=True, stop=True,
                                         skip_group_check=True)
                last.then_inc(states, 1)


def turn_and_split(nc, b, src, hi, lo, blocks):
    with ExitStack() as ctx:
        tp = ctx.enter_context(psum(nc, "ps_ts", [P, 4, 512], F32))
        with stage(nc, "turned", "hi_done", "lo_done") as (turned, hi_done, lo_done), nc.Block() as block:
            @block.tensor
            def _(pe):
                for n in range(blocks):
                    if n >= 4:
                        pe.wait_ge(lo_done, n - 3)
                    for t in range(NT):
                        last = pe.transpose(tp[:, n % 4, t * P:t * P + P], src(t, n), b.ident)
                    last.then_inc(turned, 1)

            @block.scalar
            def _(act):
                for n in range(blocks):
                    act.wait_ge(turned, n + 1)
                    act.activation(hi[:, n, :], tp[:, n % 4, 0:TOK], ACT.Copy).then_inc(hi_done, 1)

            @block.vector
            def _(dve):
                for n in range(blocks):
                    dve.wait_ge(hi_done, n + 1)
                    dve.tensor_tensor(lo[:, n, :], tp[:, n % 4, 0:TOK], hi[:, n, :].bitcast(F32),
                                      ALU.subtract).then_inc(lo_done, 1)


def merge(nc, b, a, l):
    w = at(l, a["w_in"]).rearrange("(q k p) n -> q p k n", p=P, k=4)
    wb = at(l, a["w_branch"])
    R3 = 3
    with ExitStack() as ctx:
        yhi = ctx.enter_context(sbuf(nc, "y_hi", [P, NB * 4, TOK], F32R))
        ylo = ctx.enter_context(sbuf(nc, "y_lo", [P, NB * 4, TOK], F32R))
        sg = ctx.enter_context(sbuf(nc, "merge_gate", [P, NT, 512], F32))
        turn_and_split(nc, b, lambda t, n: b.y[:, t, n // 4, (n % 4) * P:(n % 4) * P + P], yhi, ylo, NB * 4)
        acc = ctx.enter_context(psum(nc, "merge_acc", [P, 2 * NT, 512], F32))
        units = NB * 2 * R3
        with stage(nc, *[f"landed{j}" for j in range(3)], "high", "split", "multiplied", "gated", "joined",
                   "merged") as (
                *landed, high, split, multiplied, gated, joined, merged), nc.Block() as block:
            @block.sync
            def _(sp):
                for br in range(NB):
                    for cc in range(2):
                        for j in range(R3):
                            n = (br * 2 + cc) * R3 + j
                            if n >= 3:
                                sp.wait_ge(split, n - 2)
                            if j < 2:
                                c = MG + br * D + cc * 512
                                src = w[j][:, :, c:c + 512]
                            else:
                                src = wb[br].rearrange("(k p) n -> p k n", p=P)[:, :, cc * 512:cc * 512 + 512]
                            sp.dma_start(b.wraw[:, n % 3, :].rearrange("p (k n) -> p k n", k=4), src)\
                                .then_inc(landed[n % 3], 16)

            @block.scalar
            def _(act):
                def gate(c):
                    act.wait_ge(multiplied, R3 * c + 2)
                    if c >= 1:
                        act.wait_ge(joined, c)
                    act.activation(sg[:, :, :], acc[:, 0:NT, :], ACT.Sigmoid).then_inc(gated, 1)

                for n in range(units):
                    act.wait_ge(landed[n % 3], 16 * (n // 3 + 1))
                    if n >= SPL:
                        act.wait_ge(multiplied, n - SPL + 1)
                    act.activation(b.whi[:, n % SPL, :], b.wraw[:, n % 3, :], ACT.Copy).then_inc(high, 1)
                    if n % R3 == 2:
                        gate(n // R3)

            @block.vector
            def _(dve):
                def join(c):
                    br, cc = c // 2, c % 2
                    dve.wait_ge(multiplied, R3 * c + 3)
                    dve.wait_ge(gated, c + 1)
                    m = b.mg[:, :, cc * 512:cc * 512 + 512]
                    if br == 0:
                        dve.tensor_tensor(m, acc[:, NT:2 * NT, :], sg[:, :, :], ALU.mult).then_inc(joined, 1)
                    else:
                        dve.tensor_tensor(sg[:, :, :], acc[:, NT:2 * NT, :], sg[:, :, :], ALU.mult).then_inc(merged, 1)
                        dve.wait_ge(merged, c - 1)
                        dve.wait_ge(joined, c)
                        dve.tensor_tensor(m, m, sg[:, :, :], ALU.add).then_inc(joined, 1)

                for n in range(units):
                    dve.wait_ge(high, n + 1)
                    dve.tensor_tensor(b.wlo[:, n % SPL, :], b.wraw[:, n % 3, :], b.whi[:, n % SPL, :].bitcast(F32),
                                      ALU.subtract).then_inc(split, 1)
                    if n % R3 == 0 and n >= R3:
                        join(n // R3 - 1)
                join(units // R3 - 1)

            @block.tensor
            def _(pe):
                for n in range(units):
                    c, j = n // R3, n % R3
                    if c >= 1 and j == 0:
                        pe.wait_ge(gated, c)
                    if c >= 1 and j == 2:
                        pe.wait_ge(joined, c)
                    pe.wait_ge(split, n + 1)
                    for k4 in range(4):
                        cs = slice(k4 * 512, k4 * 512 + 512)
                        for t in range(NT):
                            r = slice(t * P, t * P + P)
                            if j < 2:
                                k = 4 * j + k4
                                last = product(pe, acc[:, t, :], b.hhi[:, k, r], b.hlo[:, k, r],
                                               b.whi[:, n % SPL, cs], b.wlo[:, n % SPL, cs], k == 0, k == KD - 1)
                            else:
                                k = 4 * (c // 2) + k4
                                last = product(pe, acc[:, NT + t, :], yhi[:, k, r], ylo[:, k, r],
                                               b.whi[:, n % SPL, cs], b.wlo[:, n % SPL, cs], k4 == 0, k4 == 3)
                    last.then_inc(multiplied, 1)


def out_project(nc, b, a, l):
    w = at(l, a["w_out"]).rearrange("(q k p) n -> q p k n", p=P, k=4)
    turn_and_split(nc, b, lambda t, n: b.mg[:, t, n * P:n * P + P], b.hhi, b.hlo, KD)
    with ExitStack() as ctx:
        acc = ctx.enter_context(psum(nc, "out_acc", [P, 2 * NT, 512], F32))
        gx = ctx.enter_context(sbuf(nc, "gated_out", [P, 2, NT, 512], F32))
        with stage(nc, "landed0", "landed1", "landed2", "landed3", "high", "split", "multiplied", "gated", "added") as (
                *landed, high, split, multiplied, gated, added), nc.Block() as block:
            @block.sync
            def _(sp):
                for n in range(4):
                    sp.dma_start(b.wraw[:, n, :].rearrange("p (k n) -> p k n", k=4),
                                 w[n % 2][:, :, (n // 2) * 512:(n // 2) * 512 + 512]).then_inc(landed[n], 16)

            @block.scalar
            def _(act):
                for n in range(4):
                    act.wait_ge(landed[n], 16)
                    if n >= SPL:
                        act.wait_ge(multiplied, n - SPL + 1)
                    act.activation(b.whi[:, n % SPL, :], b.wraw[:, n, :], ACT.Copy).then_inc(high, 1)

            @block.vector
            def _(dve):
                def add(c):
                    cs = slice(c * 512, c * 512 + 512)
                    dve.wait_ge(multiplied, 2 * c + 2)
                    dve.tensor_tensor(gx[:, c, 0, :], acc[:, NT * c, :], b.gate[:, 0, 0, cs], ALU.mult)\
                        .then_inc(gated, 1)
                    dve.tensor_tensor(gx[:, c, 1:3, :], acc[:, NT * c + 1:NT * c + 3, :],
                                      b.gate[:, 0, 1, cs].unsqueeze(1).to_broadcast([P, 2, 512]), ALU.mult)\
                        .then_inc(gated, 1)
                    dve.wait_ge(gated, 2 * c + 2)
                    dve.tensor_tensor(b.x[:, :, cs], b.x[:, :, cs], gx[:, c], ALU.add).then_inc(added, 1)

                for n in range(4):
                    dve.wait_ge(high, n + 1)
                    dve.tensor_tensor(b.wlo[:, n % SPL, :], b.wraw[:, n, :], b.whi[:, n % SPL, :].bitcast(F32),
                                      ALU.subtract).then_inc(split, 1)
                    if n == 2:
                        add(0)
                add(1)

            @block.tensor
            def _(pe):
                for n in range(4):
                    pe.wait_ge(split, n + 1)
                    for k4 in range(4):
                        k = 4 * (n % 2) + k4
                        cs = slice(k4 * 512, k4 * 512 + 512)
                        for t in range(NT):
                            r = slice(t * P, t * P + P)
                            last = product(pe, acc[:, NT * (n // 2) + t, :], b.hhi[:, k, r], b.hlo[:, k, r],
                                           b.whi[:, n % SPL, cs], b.wlo[:, n % SPL, cs], k == 0, k == KD - 1)
                    last.then_inc(multiplied, 1)


def key_scores(nc, b, a, l):
    w = at(l, a["peer_wq"]).rearrange("(k p) n -> p k n", p=P)
    G = 2 * PH
    with ExitStack() as ctx:
        sb = lambda n, s, dt=F32: ctx.enter_context(sbuf(nc, n, s, dt))
        ps = lambda n, s: ctx.enter_context(psum(nc, n, s, F32))
        sk = sb("subkeys", [P, 2, P])
        khi, klo = sb("k_hi", [P, 2, P], F32R), sb("k_lo", [P, 2, P], F32R)
        qhi, qlo = sb("q_hi", [P, 2, TOK], F32R), sb("q_lo", [P, 2, TOK], F32R)
        tp = ps("ps_sk", [P, 512])
        pq = ps("ps_q", [P, 2, 512])
        pss = ps("ps_s", [P, 2, 512])
        with stage(nc, *[f"landed{j}" for j in range(RAW)], "keys_in", "k_turned", "k_hi_done", "k_lo_done",
                   "high", "split", "multiplied", "q_done", "q_high", "q_split", "scored", "s_stored") as (
                *landed, keys_in, k_turned, k_hi_done, k_lo_done, high, split, multiplied, q_done, q_high, q_split,
                scored, s_stored), nc.Block() as block:
            @block.sync
            def _(sp):
                sp.dma_start(sk[:, :, :], at(l, a["peer_subkeys"]).rearrange("s n d -> n s d")).then_inc(keys_in, 16)
                for n in range(PH):
                    if n >= RAW:
                        sp.wait_ge(split, n - RAW + 1)
                    sp.dma_start(b.wraw[:, n % RAW, :].rearrange("p (k n) -> p k n", k=KD),
                                 w[:, :, n * 256:n * 256 + 256]).then_inc(landed[n % RAW], 16)

            @block.scalar
            def _(act):
                act.wait_ge(k_turned, 1)
                act.activation(khi[:, :, :].rearrange("p s n -> p (s n)"), tp[:, 0:256], ACT.Copy)\
                    .then_inc(k_hi_done, 1)

                def unit(n):
                    act.wait_ge(landed[n % RAW], 16 * (n // RAW + 1))
                    if n >= SPL:
                        act.wait_ge(q_done, 2 * (n - SPL) + 2)
                    act.activation(b.whi[:, n % SPL, :], b.wraw[:, n % RAW, :], ACT.Copy).then_inc(high, 1)

                unit(0)
                for g in range(G):
                    if g % 2 == 0 and g // 2 + 1 < PH:
                        unit(g // 2 + 1)
                    act.wait_ge(q_done, g + 1)
                    if g >= 2:
                        act.wait_ge(scored, g - 1)
                    act.activation(qhi[:, g % 2, :], pq[:, g % 2, 0:TOK], ACT.Copy).then_inc(q_high, 1)

            @block.vector
            def _(dve):
                dve.wait_ge(k_hi_done, 1)
                dve.tensor_tensor(klo[:, :, :].rearrange("p s n -> p (s n)"), tp[:, 0:256],
                                  khi[:, :, :].rearrange("p s n -> p (s n)").bitcast(F32), ALU.subtract)\
                    .then_inc(k_lo_done, 1)

                def unit(n):
                    dve.wait_ge(high, n + 1)
                    dve.tensor_tensor(b.wlo[:, n % SPL, :], b.wraw[:, n % RAW, :], b.whi[:, n % SPL, :].bitcast(F32),
                                      ALU.subtract).then_inc(split, 1)

                def store(g):
                    dve.wait_ge(scored, g + 1)
                    dve.tensor_copy(b.sall[:, :, g, :], pss[:, g % 2, 0:TOK].rearrange("p (t n) -> p t n", t=NT))\
                        .then_inc(s_stored, 1)

                unit(0)
                for g in range(G):
                    if g % 2 == 0 and g // 2 + 1 < PH:
                        unit(g // 2 + 1)
                    dve.wait_ge(q_high, g + 1)
                    dve.tensor_tensor(qlo[:, g % 2, :], pq[:, g % 2, 0:TOK], qhi[:, g % 2, :].bitcast(F32),
                                      ALU.subtract).then_inc(q_split, 1)
                    if g >= 1:
                        store(g - 1)
                store(G - 1)

            @block.tensor
            def _(pe):
                pe.wait_ge(keys_in, 16)
                for i in range(2):
                    last = pe.transpose(tp[:, i * P:i * P + P], sk[:, i, :], b.ident)
                last.then_inc(k_turned, 1)

                def query(g):
                    pe.wait_ge(split, g // 2 + 1)
                    if g >= 2:
                        pe.wait_ge(q_split, g - 1)
                    u = (g // 2) % SPL
                    for k in range(KD):
                        c = slice(k * 256 + (g % 2) * P, k * 256 + (g % 2) * P + P)
                        last = product(pe, pq[:, g % 2, 0:TOK], b.whi[:, u, c], b.wlo[:, u, c],
                                       b.hhi[:, k, :], b.hlo[:, k, :], k == 0, k == KD - 1)
                    last.then_inc(q_done, 1)

                def score(g):
                    pe.wait_ge(q_split, g + 1)
                    pe.wait_ge(k_lo_done, 1)
                    if g >= 2:
                        pe.wait_ge(s_stored, g - 1)
                    for t in range(NT):
                        r = slice(t * P, t * P + P)
                        last = product(pe, pss[:, g % 2, r], qhi[:, g % 2, r], qlo[:, g % 2, r],
                                       khi[:, g % 2, :], klo[:, g % 2, :], True, True)
                    last.then_inc(scored, 1)

                query(0)
                for g in range(1, G):
                    query(g)
                    score(g - 1)
                score(G - 1)


def top_keys(nc, b, t):
    G = 2 * PH
    with ExitStack() as ctx:
        sb = lambda n, s, dt=F32: ctx.enter_context(sbuf(nc, n, s, dt))
        s = sb("tile_scores", [P, G, NK])
        v = sb("top_vals", [P, G, TOPK])
        ix = sb("top_index", [P, G, TOPK], U32)
        ixf = sb("top_index_f", [P, G, TOPK])
        cand = sb("sums", [P, PH, TOPK * TOPK])
        best = sb("best", [P, PH, TOPK])
        pos = sb("best_pos", [P, PH, TOPK], U32)
        half = sb("pos_half", [P, 2, SLOTS], U32)
        halff = sb("pos_half_f", [P, 2, SLOTS])
        eq = sb("equal", [P, 2, SLOTS, TOPK])
        out = sb("slots", [P, 3, SLOTS])
        e = sb("exps", [P, PH, TOPK])
        st = sb("gate_stats", [P, 2, PH])
        ps = ctx.enter_context(psum(nc, "ps_slots", [P, 512], F32))
        with stage(nc, "dve_done", "ask", "expd", "ready", "turned") as (dve_done, ask, expd, ready, turned), \
                nc.Block() as block:
            @block.scalar
            def _(act):
                act.wait_ge(ask, 1)
                act.activation(e[:, :, :], e[:, :, :], ACT.Exp).then_inc(expd, 1)

            @block.tensor
            def _(pe):
                pe.wait_ge(ready, 1)
                for i in range(3):
                    last = pe.transpose(ps[:, i * P:i * P + P], out[:, i, :], b.ident)
                last.then_inc(turned, 1)

            @block.vector
            def _(dve):
                link = Chain(dve, dve_done)

                def top16(vals, index, src, n):
                    for r in range(2):
                        o = slice(8 * r, 8 * r + 8)
                        for g in range(n):
                            last = dve.max(vals[:, g, o], src[:, g, :])
                        link(last)
                        for g in range(n):
                            last = dve.max_index(index[:, g, o], vals[:, g, o], src[:, g, :])
                        link(last)
                        if r == 0:
                            for g in range(n):
                                last = dve.match_replace(src[:, g, :], vals[:, g, o], src[:, g, :], -3.0e38)
                            link(last)

                link(dve.tensor_copy(s[:, :, :], b.sall[:, bass.ds(t, 1)].rearrange("p a g n -> p (a g) n")))
                top16(v, ix, s, G)
                link(dve.tensor_copy(ixf[:, :, :], ix[:, :, :]))
                for h in range(PH):
                    last = dve.tensor_tensor(cand[:, h, :].rearrange("p (i j) -> p i j", i=TOPK),
                                             v[:, 2 * h, :].unsqueeze(2).to_broadcast([P, TOPK, TOPK]),
                                             v[:, 2 * h + 1, :].unsqueeze(1).to_broadcast([P, TOPK, TOPK]), ALU.add)
                link(last)
                top16(best, pos, cand, PH)
                dve.tensor_tensor(e[:, :, :], best[:, :, :], best[:, :, 0:1].to_broadcast([P, PH, TOPK]),
                                  ALU.subtract).then_inc(ask, 1)
                flat = pos[:, :, :].rearrange("p h k -> p (h k)")
                link(dve.tensor_scalar(half[:, 0, :], flat, 4, None, ALU.logical_shift_right))
                link(dve.tensor_scalar(half[:, 1, :], flat, 15, None, ALU.bitwise_and))
                link(dve.tensor_copy(halff[:, :, :], half[:, :, :]))
                iota = b.cst[:, C_IO:C_IO + TOPK].unsqueeze(1).to_broadcast([P, SLOTS, TOPK])
                for i in range(2):
                    last = dve.tensor_tensor(eq[:, i], halff[:, i, :].unsqueeze(2).to_broadcast([P, SLOTS, TOPK]),
                                             iota, ALU.is_equal)
                link(last)
                for i in range(2):
                    src = ixf[:, i::2, :].unsqueeze(2).to_broadcast([P, PH, TOPK, TOPK])
                    q = eq[:, i].rearrange("p (h k) j -> p h k j", h=PH)
                    last = dve.tensor_tensor(q, q, src, ALU.mult)
                link(last)
                for i in range(2):
                    last = dve.tensor_reduce(out[:, 1 + i, :], eq[:, i], AX_X, ALU.add)
                link(last)
                dve.wait_ge(expd, 1)
                link(dve.tensor_reduce(st[:, 0, :], e[:, :, :], AX_X, ALU.add))
                link(dve.reciprocal(st[:, 1, :], st[:, 0, :]))
                dve.tensor_tensor(out[:, 0, :].rearrange("p (h k) -> p h k", h=PH), e[:, :, :],
                                  st[:, 1, :].unsqueeze(2).to_broadcast([P, PH, TOPK]), ALU.mult).then_inc(ready, 1)
                dve.wait_ge(turned, 1)
                link(dve.tensor_copy(b.slots[:, bass.ds(t, 1)].rearrange("p a i n -> p (a i n)"), ps[:, 0:3 * P]))


def gate_matrix(nc, b, a, t):
    GROUP = 4
    with ExitStack() as ctx:
        sb = lambda n, s: ctx.enter_context(sbuf(nc, n, s, F32))
        tile = sb("slots_tile", [P, 3, P])
        oh1 = sb("one_hot_1", [P, 2, GROUP, NK])
        oh2 = sb("one_hot_2", [P, 2, GROUP, NK])
        gm = sb("gates_tile", [P, NK, P])
        ps = ctx.enter_context(psum(nc, "ps_gates", [P, 2, 512], F32))
        G = P // GROUP
        with stage(nc, "slots_in", "hot", "summed", "stored", "written") as (slots_in, hot, summed, stored, written), \
                nc.Block() as block:
            @block.vector
            def _(dve):
                dve.tensor_copy(tile[:, :, :].rearrange("p i n -> p (i n)"),
                                b.slots[:, bass.ds(t, 1)].rearrange("p a i n -> p (a i n)")).then_inc(slots_in, 1)
                dve.wait_ge(slots_in, 1)
                iota = b.cst[:, C_IO:C_IO + NK]
                for g in range(G):
                    if g >= 2:
                        dve.wait_ge(summed, g - 1)
                    for i in range(GROUP):
                        n = g * GROUP + i
                        dve.tensor_scalar(oh1[:, g % 2, i, :], iota, tile[:, 1, n:n + 1], tile[:, 0, n:n + 1],
                                          ALU.is_equal, ALU.mult)
                        last = dve.tensor_scalar(oh2[:, g % 2, i, :], iota, tile[:, 2, n:n + 1], None, ALU.is_equal)
                    last.then_inc(hot, 1)

            @block.tensor
            def _(pe):
                for g in range(G):
                    pe.wait_ge(hot, g + 1)
                    if g >= 2:
                        pe.wait_ge(stored, g - 1)
                    for i in range(GROUP):
                        last = pe.matmul(ps[:, g % 2, i * NK:i * NK + NK], oh1[:, g % 2, i, :], oh2[:, g % 2, i, :],
                                         start=True, stop=True, skip_group_check=True)
                    last.then_inc(summed, 1)

            @block.scalar
            def _(act):
                for g in range(G):
                    act.wait_ge(summed, g + 1)
                    act.activation(gm[:, :, g * GROUP:(g + 1) * GROUP].rearrange("p i n -> p n i"),
                                   ps[:, g % 2, :].rearrange("p (n i) -> p n i", n=GROUP), ACT.Copy)\
                        .then_inc(stored, 1)

            @block.sync
            def _(sp):
                sp.wait_ge(stored, G)
                dst = b.gates[bass.ds(t, 1)].rearrange("a i p n -> p (a i) n")
                for q in range(4):
                    sp.dma_start(dst[:, 32 * q:32 * q + 32, :], gm[:, 32 * q:32 * q + 32, :]).then_inc(written, 16)
                sp.wait_ge(written, 64)


def experts(nc, b, a, l):
    E = NK
    ut = at(l, a["peer_u"]).rearrange("(p i) d -> i p d", i=E)
    vt = at(l, a["peer_v"]).rearrange("(p i) d -> i p d", i=E)
    gt = b.gates.rearrange("t i p n -> i p t n")
    with ExitStack() as ctx:
        sb = lambda n, s, dt=F32: ctx.enter_context(sbuf(nc, n, s, dt))
        ps = lambda n, s: ctx.enter_context(psum(nc, n, s, F32))
        u, v = sb("u_rows", [P, 2, D]), sb("v_rows", [P, 2, D])
        g = sb("gate_block", [P, 2, NT, P])
        uhi, ulo = sb("u_hi", [P, 2, KD * P], F32R), sb("u_lo", [P, 2, KD * P], F32R)
        vhi, vlo = sb("v_hi", [P, 2, D], F32R), sb("v_lo", [P, 2, D], F32R)
        act_out = sb("gelu_out", [P, 2, TOK])
        wt = sb("weights", [P, 2, TOK])
        whi, wlo = sb("w_hi", [P, 2, TOK], F32R), sb("w_lo", [P, 2, TOK], F32R)
        gx = sb("gated_out", [P, NT, D])
        acc = ps("expert_acc", [P, NT * 2, 512])
        pa = ps("ps_act", [P, 512])
        tp = ps("ps_ut", [P, 512])
        with stage(nc, "u_in0", "u_in1", "v_in0", "v_in1", "g_in0", "g_in1", "u_turned", "u_high", "u_low",
                   "scored", "gelu_done", "weighed", "w_high", "w_low", "v_high", "v_low", "summed", "gated",
                   "added") as (
                u_in0, u_in1, v_in0, v_in1, g_in0, g_in1, u_turned, u_high, u_low, scored, gelu_done, weighed,
                w_high, w_low, v_high, v_low, summed, gated, added), nc.Block() as block:
            u_in, v_in, g_in = (u_in0, u_in1), (v_in0, v_in1), (g_in0, g_in1)

            @block.sync
            def _(sp):
                def load(e, par, first):
                    if not first:
                        sp.wait_ge(u_turned, e * 2 - 2)
                    sp.dma_start(u[:, par, :], ut[bass.ds(e, 1)].rearrange("a p d -> (a p) d")).then_inc(u_in[par], 16)
                    if not first:
                        sp.wait_ge(v_low, e - 1)
                    sp.dma_start(v[:, par, :], vt[bass.ds(e, 1)].rearrange("a p d -> (a p) d")).then_inc(v_in[par], 16)
                    if not first:
                        sp.wait_ge(weighed, e - 1)
                    sp.dma_start(g[:, par], gt[bass.ds(e, 1)].rearrange("a p t n -> (a p) t n")).then_inc(g_in[par], 16)

                load(0, 0, True)
                load(1, 1, True)
                with sp.Fori(1, E // 2) as pair:
                    e = pair * 2
                    load(e, 0, False)
                    load(e + 1, 1, False)

            def count16(e, par):
                return (e // 2 + 1) * 16 if isinstance(e, int) else (e - par) * 8 + 16

            @block.scalar
            def _(act):
                def turn_high(e, par, hf):
                    act.wait_ge(u_turned, e * 2 + (hf + 1))
                    c = slice(hf * 512, hf * 512 + 512)
                    act.activation(uhi[:, par, c], tp[:, :], ACT.Copy).then_inc(u_high, 1)

                def v_part(e, par, first):
                    act.wait_ge(v_in[par], count16(e, par))
                    if not first:
                        act.wait_ge(summed, e - 1)
                    act.activation(vhi[:, par, :], v[:, par, :], ACT.Copy).then_inc(v_high, 1)

                def step(e, par, first, last):
                    if not last:
                        turn_high(e + 1, 1 - par, 0)
                    v_part(e, par, first)
                    act.wait_ge(scored, e + 1)
                    act.activation(act_out[:, par, :], pa[:, 0:TOK], ACT.Gelu_apprx_tanh).then_inc(gelu_done, 1)
                    if not last:
                        turn_high(e + 1, 1 - par, 1)
                    act.wait_ge(weighed, e + 1)
                    act.activation(whi[:, par, :], wt[:, par, :], ACT.Copy).then_inc(w_high, 1)

                turn_high(0, 0, 0)
                turn_high(0, 0, 1)
                step(0, 0, True, False)
                step(1, 1, True, False)
                with act.Fori(1, E // 2 - 1) as pair:
                    e = pair * 2
                    step(e, 0, False, False)
                    step(e + 1, 1, False, False)
                step(E - 2, 0, False, False)
                step(E - 1, 1, False, True)

            @block.vector
            def _(dve):
                def turn_low(e, par, hf):
                    dve.wait_ge(u_high, e * 2 + (hf + 1))
                    c = slice(hf * 512, hf * 512 + 512)
                    dve.tensor_tensor(ulo[:, par, c], tp[:, :], uhi[:, par, c].bitcast(F32), ALU.subtract)\
                        .then_inc(u_low, 1)

                def step(e, par, last):
                    if not last:
                        turn_low(e + 1, 1 - par, 0)
                    dve.wait_ge(v_high, e + 1)
                    dve.tensor_tensor(vlo[:, par, :], v[:, par, :], vhi[:, par, :].bitcast(F32), ALU.subtract)\
                        .then_inc(v_low, 1)
                    dve.wait_ge(gelu_done, e + 1)
                    dve.wait_ge(g_in[par], count16(e, par))
                    dve.tensor_tensor(wt[:, par, :], act_out[:, par, :], g[:, par].rearrange("p t n -> p (t n)"),
                                      ALU.mult).then_inc(weighed, 1)
                    if not last:
                        turn_low(e + 1, 1 - par, 1)
                    dve.wait_ge(w_high, e + 1)
                    dve.tensor_tensor(wlo[:, par, :], wt[:, par, :], whi[:, par, :].bitcast(F32), ALU.subtract)\
                        .then_inc(w_low, 1)

                turn_low(0, 0, 0)
                turn_low(0, 0, 1)
                with dve.Fori(0, E // 2 - 1) as pair:
                    e = pair * 2
                    step(e, 0, False)
                    step(e + 1, 1, False)
                step(E - 2, 0, False)
                step(E - 1, 1, True)
                dve.wait_ge(summed, E)
                dve.tensor_tensor(gx[:, 0, :], acc[:, 0:2, :].rearrange("p c n -> p (c n)"), b.gate[:, 1, 0, :],
                                  ALU.mult).then_inc(gated, 1)
                dve.tensor_tensor(gx[:, 1:3, :], acc[:, 2:6, :].rearrange("p (t c) n -> p t (c n)", c=2),
                                  b.gate[:, 1, 1, :].unsqueeze(1).to_broadcast([P, 2, D]), ALU.mult).then_inc(gated, 1)
                dve.wait_ge(gated, 2)
                dve.tensor_tensor(b.x[:, :, :], b.x[:, :, :], gx[:, :, :], ALU.add).then_inc(added, 1)

            @block.tensor
            def _(pe):
                def turn(e, par, hf, first):
                    if hf == 0:
                        pe.wait_ge(u_in[par], count16(e, par))
                    if not first:
                        pe.wait_ge(u_low, e * 2 + hf)
                    for i in range(4):
                        k = 4 * hf + i
                        last = pe.transpose(tp[:, i * P:i * P + P], u[:, par, k * P:k * P + P], b.ident)
                    last.then_inc(u_turned, 1)

                def score(e, par, first):
                    pe.wait_ge(u_low, e * 2 + 2)
                    if not first:
                        pe.wait_ge(gelu_done, e)
                    for k in range(KD):
                        c = slice(k * P, k * P + P)
                        last = product(pe, pa[:, 0:TOK], uhi[:, par, c], ulo[:, par, c], b.hhi[:, k, :],
                                       b.hlo[:, k, :], k == 0, k == KD - 1)
                    last.then_inc(scored, 1)

                def add(e, par, first):
                    pe.wait_ge(w_low, e + 1)
                    for t in range(NT):
                        r = slice(t * P, t * P + P)
                        for c in range(2):
                            cs = slice(c * 512, c * 512 + 512)
                            last = product(pe, acc[:, 2 * t + c, :], whi[:, par, r], wlo[:, par, r],
                                           vhi[:, par, cs], vlo[:, par, cs], first, False)
                    last.then_inc(summed, 1)

                turn(0, 0, 0, True)
                turn(0, 0, 1, False)
                turn(1, 1, 0, False)
                score(0, 0, True)
                turn(1, 1, 1, False)
                turn(2, 0, 0, False)
                score(1, 1, False)
                turn(2, 0, 1, False)
                add(0, 0, True)
                with pe.Fori(1, E // 2 - 1) as pair:
                    e = pair * 2
                    for d in range(2):
                        turn(e + (d + 1), 1 - d, 0, False)
                        score(e + d, d, False)
                        turn(e + (d + 1), 1 - d, 1, False)
                        add(e + (d - 1), 1 - d, False)
                turn(E - 1, 1, 0, False)
                score(E - 2, 0, False)
                turn(E - 1, 1, 1, False)
                add(E - 3, 1, False)
                score(E - 1, 1, False)
                add(E - 2, 0, False)
                add(E - 1, 1, False)


def final(nc, b, a):
    with ExitStack() as ctx:
        gf = ctx.enter_context(sbuf(nc, "final_gain", [P, D], F32))
        y = ctx.enter_context(sbuf(nc, "final_out", [P, NT, D], F32))
        st = ctx.enter_context(sbuf(nc, "final_stats", [P, 4, NT], F32))
        with stage(nc, "loaded", "squared", "dve_done", "rooted", "normed", "written") as (
                loaded, squared, dve_done, rooted, normed, written), nc.Block() as block:
            @block.sync
            def _(sp):
                sp.dma_start(gf[:, :], a["norm_f"].partition_broadcast(P)).then_inc(loaded, 16)
                sp.wait_ge(normed, NT)
                sp.dma_start(a["o_prompt"][0], y[:, 0, :]).then_inc(written, 16)
                sp.dma_start(a["o_sample"][0].rearrange("(t p) d -> p t d", p=P), y[:, 1:3, :]).then_inc(written, 16)
                sp.wait_ge(written, 32)

            @block.scalar
            def _(act):
                for t in range(NT):
                    act.activation(y[:, t, :], b.x[:, t, :], ACT.Square, accum_out=st[:, 0, t:t + 1])\
                        .then_inc(squared, 1)
                act.wait_ge(dve_done, 1)
                act.activation(st[:, 2, :], st[:, 1, :], ACT.Sqrt).then_inc(rooted, 1)

            @block.vector
            def _(dve):
                link = Chain(dve, dve_done)
                dve.wait_ge(squared, NT)
                link(dve.tensor_scalar(st[:, 1, :], st[:, 0, :], 1.0 / D, EPS, ALU.mult, ALU.add))
                dve.wait_ge(rooted, 1)
                link(dve.reciprocal(st[:, 3, :], st[:, 2, :]))
                dve.wait_ge(loaded, 16)
                for t in range(NT):
                    dve.scalar_tensor_tensor(y[:, t, :], b.x[:, t, :], st[:, 3, t:t + 1], gf[:, :],
                                             ALU.mult, ALU.mult).then_inc(normed, 1)


def program(nc, a):
    with ExitStack() as ctx:
        def sb(name, shape, dt=F32):
            return ctx.enter_context(sbuf(nc, name, shape, dt))

        b = Buffers()
        b.x = sb("x", [P, NT, D])
        b.cst = sb("cst", [P, C_ALL])
        b.ident = b.cst[:, C_ID:C_ID + P]
        b.cnd = sb("conditions", [P, KD, P], F32R)
        b.hhi, b.hlo = sb("h_hi", [P, KD, TOK], F32R), sb("h_lo", [P, KD, TOK], F32R)
        b.scale, b.shift = sb("scale", [P, 2, KD, 2]), sb("shift", [P, 2, KD, 2])
        b.gate = sb("gates_b", [P, 2, 2, D])
        b.bias = nc.dram_tensor("bias_scratch", (DEPTH, P, 2, H, LAT), F32, kind="Internal").ap()
        b.gates = nc.dram_tensor("gate_scratch", (NT, NK, P, P), F32, kind="Internal").ap()

        @contextmanager
        def stream():
            with sbuf(nc, "w_raw", [P, RAW, UNIT], F32) as b.wraw, \
                    sbuf(nc, "w_high", [P, SPL, UNIT], F32R) as b.whi, \
                    sbuf(nc, "w_low", [P, SPL, UNIT], F32R) as b.wlo:
                yield

        setup(nc, b, a)
        with nc.Fori(0, DEPTH) as l:
            with stream():
                modulation(nc, b, a, l)
            norm(nc, b, 0)
            with sbuf(nc, "y", [P, NT, NB, BW], F32) as b.y:
                with sbuf(nc, "proj", [P, NT, MIX_W], F32) as b.proj:
                    with stream():
                        project(nc, b, a, l)
                    rotary(nc, b)
                    attention(nc, b, a, l, True)
                    attention(nc, b, a, l, False)
                    retention(nc, b, a, l)
                with sbuf(nc, "merged", [P, NT, D], F32) as b.mg, stream():
                    merge(nc, b, a, l)
                    out_project(nc, b, a, l)
            norm(nc, b, 1)
            with sbuf(nc, "slots_t", [P, NT, 3, P], F32) as b.slots:
                with sbuf(nc, "key_scores", [P, NT, 2 * PH, NK], F32) as b.sall:
                    with stream():
                        key_scores(nc, b, a, l)
                    with nc.Fori(0, NT) as t:
                        top_keys(nc, b, t)
                with nc.Fori(0, NT) as t:
                    gate_matrix(nc, b, a, t)
            experts(nc, b, a, l)
        final(nc, b, a)


INPUTS = ["x_prompt", "x_sample", "c", "cache_diff_k", "cache_diff_v", "cache_na_k", "cache_na_v", "state_ret",
          "c_ctx", "w_mod", "b_mod", "norm1", "w_in", "diff_lambda", "diff_gn", "ret_decay", "ret_gn", "na_pad",
          "w_branch", "w_out", "norm2", "peer_wq", "peer_subkeys", "peer_u", "peer_v", "norm_f"]
OUTPUTS = [("o_prompt", (1, CTX, D)), ("o_sample", (1, LAT, D)),
           ("o_diff_k", (1, DEPTH, H, CTX, DH)), ("o_diff_v", (1, DEPTH, H, CTX, DH)),
           ("o_na_k", (1, DEPTH, H, CTX, DH)), ("o_na_v", (1, DEPTH, H, CTX, DH)),
           ("o_state", (1, DEPTH, 2, H, 64, DH))]


def kernel(**inputs):
    import concourse.bacc as bacc
    from concourse.bass_utils import run_bass_kernel_spmd

    inputs["na_pad"] = np.pad(np.asarray(inputs["na_bias"]), ((0, 0), (0, 0), (0, 0), (48, 48)))
    nc = bacc.Bacc("TRN2", target_bir_lowering=False, num_devices=1)
    arrays, a = {}, {}
    for name in INPUTS:
        v = np.ascontiguousarray(inputs[name])
        arrays[name + "_in"] = v
        a[name] = nc.dram_tensor(name + "_in", v.shape, mybir.dt.from_np(v.dtype), kind="ExternalInput").ap()
    for name, shape in OUTPUTS:
        a[name] = nc.dram_tensor(name, shape, F32, kind="ExternalOutput").ap()
    a["const"] = nc.inline_tensor(constants(), name="constants").ap()
    program(nc, a)
    r = run_bass_kernel_spmd(nc, [arrays], core_ids=[0])
    return tuple(r.results[0][name] for name, _ in OUTPUTS)
```

```python
from contextlib import ExitStack, contextmanager
import math

import numpy as np

import concourse.bass as bass
from concourse import mybir

F32 = mybir.dt.float32
F32R = mybir.dt.float32r
U32 = mybir.dt.uint32
ALU = mybir.AluOpType
ACT = mybir.ActivationFunctionType
AX_X = mybir.AxisListType.X

P = 128
D = 1024
KD = D // P
DEPTH = 2
NT = 3
TOK = NT * P
LAT = 256
CTX = 128
GRID_W = 64
H = 4
DH = 128
EPS = 1e-6
NEG = -1e30

QA, KA, VA, QB, KB, VB, GB, QC, KC, VC, MG = 0, 512, 1024, 1536, 1792, 2048, 2560, 3584, 4096, 4608, 5120
MIX_W = MG
IN_TOTAL = 8192
NB = 3
BW = 512

PH = 8
NK = 128
TOPK = 16
SLOTS = PH * TOPK

UNIT = 2048
RAW = 4
SPL = 2

C_ID = 0
C_D0 = C_ID + P
C_M0 = C_D0 + 4 * 128
C_IO = C_M0 + 2 * 128
C_NM = C_IO + NK
C_QE = C_NM + 64
C_KE = C_QE + 512
C_COS = C_KE + 2
C_SIN = C_COS + 128
C_LAM = C_SIN + 128
C_ST = C_LAM + 2 * DEPTH
C_DS = C_ST + TOPK
C_EPS = C_DS + TOPK
C_ALL = C_EPS + 1

MOD_CHUNKS = 6 * D // 512
MOD_BESIDE = 3

ROWS = [TOPK // (i + 1) for i in range(TOPK)]
STARTS = [sum(ROWS[:i]) for i in range(TOPK)]
NSUM = sum(ROWS)


def constants():
    c = np.zeros((P, C_ALL), np.float32)
    i = np.arange(P)
    c[:, C_ID:C_ID + P] = np.eye(P)
    diff = (i[None, :] - i[:, None]).astype(np.float64)
    c[:, C_D0:C_D0 + 128] = np.maximum(diff, 0)
    c[:, C_D0 + 128:C_D0 + 256] = 128 + diff
    c[:, C_D0 + 256:C_D0 + 384] = np.maximum(-diff, 0)
    c[:, C_D0 + 384:C_D0 + 512] = 128 - diff
    c[:, C_M0:C_M0 + 128] = diff >= 0
    c[:, C_M0 + 128:C_M0 + 256] = diff <= 0
    c[:, C_IO:C_IO + NK] = np.arange(NK)[None, :]
    cq, ck = i % GRID_W, np.arange(GRID_W)
    cs = np.clip(cq - 8, 0, GRID_W - 16)[:, None]
    c[:, C_NM:C_NM + 64] = np.where((ck >= cs) & (ck < cs + 16), 0.0, NEG)
    c[:, C_QE:C_QE + 256] = np.arange(256) + 1
    c[:, C_QE + 256:C_QE + 512] = LAT - np.arange(256)
    c[:, C_KE] = CTX - 1 - i
    c[:, C_KE + 1] = i
    half = 32
    freqs = np.float32(10000.0) ** (-np.arange(0, half, 2, dtype=np.float32) / np.float32(half))
    for t in range(2):
        tok = t * P + i
        for a, pos in enumerate((tok // GRID_W, tok % GRID_W)):
            ang = (pos.astype(np.float32)[:, None] * freqs).astype(np.float32).astype(np.float64)
            o = t * 64 + a * 32
            c[:, C_COS + o:C_COS + o + 16] = c[:, C_COS + o + 16:C_COS + o + 32] = np.cos(ang)
            c[:, C_SIN + o:C_SIN + o + 16] = -np.sin(ang)
            c[:, C_SIN + o + 16:C_SIN + o + 32] = np.sin(ang)
    c[:, C_ST:C_ST + TOPK] = STARTS
    c[:, C_DS:C_DS + TOPK] = np.diff([0] + STARTS)
    c[:, C_EPS] = EPS
    for l in range(DEPTH):
        lam = 0.8 - 0.6 * math.exp(-0.3 * l)
        c[:, C_LAM + 2 * l] = lam
        c[:, C_LAM + 2 * l + 1] = 1.0 - lam
    return c


def sbuf(nc, name, shape, dt=F32):
    return nc.sbuf_tensor(f"{name}_{nc.next_id()}", shape, dt)


def psum(nc, name, shape, dt=F32):
    return nc.psum_tensor(f"{name}_{nc.next_id()}", shape, dt)


class Chain:

    def __init__(self, eng, sem):
        self.eng, self.sem, self.n = eng, sem, 0

    def __call__(self, ins):
        self.n += 1
        ins.then_inc(self.sem, 1)
        self.eng.wait_ge(self.sem, self.n)


@contextmanager
def stage(nc, *names, also=()):
    with ExitStack() as ctx:
        sems = [ctx.enter_context(nc.semaphore(f"{n}_{nc.next_id()}")) for n in names]
        yield sems
        for s in [*sems, *also]:
            nc.sync.sem_clear(s)
        nc.all_engine_barrier()


@contextmanager
def early(nc):
    with ExitStack() as ctx:
        yield [ctx.enter_context(nc.semaphore(f"landed{j}_{nc.next_id()}")) for j in range(RAW)]


class Buffers:
    pass


def mixed(ap):
    return ap.rearrange("p (i k r) -> p k i r", i=4, k=KD)


def blocks(ap):
    return ap.rearrange("p (k i r) -> p k i r", i=4, k=KD)


def at(l, ap):
    names = " ".join("bcdefg"[:len(ap.shape) - 1])
    first = names.split(" ")[0]
    return ap[bass.ds(l, 1)].rearrange(f"a {names} -> (a {first}) {names[len(first) + 1:]}".strip())


def product(pe, out, ah, al, bh, bl, first, last):
    pe.matmul(out, ah, bh, start=first, stop=False, skip_group_check=True)
    pe.matmul(out, ah, bl, start=False, stop=False, skip_group_check=True)
    return pe.matmul(out, al, bh, start=False, stop=last, skip_group_check=True)



def high_unit(act, b, landed, multiplied, high, n, j):
    act.wait_ge(landed[j % RAW], ((n + j) // RAW + 1) * 16 if isinstance(n, int) else n * (16 // RAW) + 16)
    act.wait_ge(multiplied, n + (j + 1))
    act.activation(b.whi[:, j % SPL, :], b.wraw[:, j % RAW, :], ACT.Copy).then_inc(high, 1)


def low_unit(dve, b, high, split, n, j):
    dve.wait_ge(high, n + (j + 1))
    dve.tensor_tensor(b.wlo[:, j % SPL, :], b.wraw[:, j % RAW, :], b.whi[:, j % SPL, :].bitcast(F32),
                      ALU.subtract).then_inc(split, 1)



def load_modulation(sp, b, a, l, chunks, landed, used):
    w = at(l, a["w_mod"]).rearrange("(q k p) n -> q p k n", p=P, k=4)
    for n in range(2 * chunks):
        if n >= RAW:
            sp.wait_ge(used, n - RAW + 1)
        sp.dma_start(b.wraw[:, n % RAW, :].rearrange("p (k n) -> p k n", k=4),
                     w[n % 2][:, :, (n // 2) * 512:(n // 2) * 512 + 512]).then_inc(landed[n % RAW], 16)


def multiply_modulation(pe, b, acc, chunk, landed, used, kept):
    if chunk >= 2:
        pe.wait_ge(kept, chunk - 1)
    for k in range(KD):
        n = 2 * chunk + k // 4
        if k % 4 == 0:
            pe.wait_ge(landed[n % RAW], 16 * (n // RAW + 1))
        last = pe.matmul(acc[0:2, chunk % 2, :], b.cnd[:, k, :], b.wraw[:, n % RAW, (k % 4) * 512:(k % 4) * 512 + 512],
                         start=(k == 0), stop=(k == KD - 1), skip_group_check=True)
        if k % 4 == 3:
            last.then_inc(used, 1)


def keep_modulation(act, rows, acc, chunk, used, kept, written):
    act.wait_ge(used, 2 * chunk + 2)
    if chunk >= 2:
        act.wait_ge(written[chunk % 2], 16 * (chunk // 2))
    act.activation(rows[:, chunk % 2, :], acc[0:2, chunk % 2, :], ACT.Copy).then_inc(kept, 1)


def store_modulation(eng, b, rows, chunk, kept, written):
    eng.wait_ge(kept, chunk + 1)
    eng.dma_start(b.mods[:, chunk * 512:chunk * 512 + 512], rows[:, chunk % 2, :]).then_inc(written[chunk % 2], 16)


def setup(nc, b, a):
    with ExitStack() as ctx:
        cond = ctx.enter_context(sbuf(nc, "cond", [16, P], F32))
        rows = ctx.enter_context(sbuf(nc, "mod_rows", [2, 2, 512], F32))
        ps = ctx.enter_context(psum(nc, "ps_setup", [P, 512], F32))
        acc = ctx.enter_context(psum(nc, "mod_acc", [P, 2, 512], F32))
        with stage(nc, *[f"landed{j}" for j in range(RAW)], "used", "kept", "written0", "written1", "loaded",
                   "silu_done", "turned", "copied", "tokens_in", "biases") as (
                *landed, used, kept, written0, written1, loaded, silu_done, turned, copied, tokens_in,
                biases), nc.Block() as block:
            written = (written0, written1)

            def load_tokens(eng):
                eng.dma_start(b.x[:, 0, :], a["x_prompt"][0]).then_inc(tokens_in, 16)
                eng.dma_start(b.x[:, 1:3, :], a["x_sample"][0].rearrange("(t p) d -> p t d", p=P))\
                    .then_inc(tokens_in, 16)

            def expand_biases(eng, l, r):
                for h in range(H):
                    table = a["na_pad"][l, h, 7 - r:11 - r, :]
                    src = bass.AP(tensor=table.tensor, offset=table.offset + 63, ap=[[127, 4], [-1, 64], [1, 64]])
                    dst = b.bias[l, 64 * (r % 2):64 * (r % 2) + 64, r // 2, h, :]
                    eng.dma_start(dst.rearrange("p (j n) -> j p n", j=4), src).then_inc(biases, 16)

            @block.sync
            def _(sp):
                sp.dma_start(cond[0:KD, :], a["c_ctx"].rearrange("(k p) -> k p", p=P)).then_inc(loaded, 16)
                sp.dma_start(cond[KD:16, :], a["c"].rearrange("a (k p) -> (a k) p", p=P)).then_inc(loaded, 16)
                sp.dma_start(b.cst[:, :], a["const"]).then_inc(loaded, 16)
                load_modulation(sp, b, a, 0, MOD_CHUNKS, landed, used)

            @block.tensor
            def _(pe):
                pe.wait_ge(silu_done, 1)
                pe.transpose(ps[:, 0:16], cond[:, :], b.ident[0:16, 0:16]).then_inc(turned, 1)
                pe.wait_ge(copied, 1)
                for chunk in range(MOD_CHUNKS):
                    multiply_modulation(pe, b, acc, chunk, landed, used, kept)

            @block.scalar
            def _(act):
                act.wait_ge(loaded, 3 * 16)
                act.activation(cond[:, :], cond[:, :], ACT.Silu).then_inc(silu_done, 1)
                for chunk in range(MOD_CHUNKS):
                    keep_modulation(act, rows, acc, chunk, used, kept, written)
                    store_modulation(act, b, rows, chunk, kept, written)
                    if 1 <= chunk <= 4 * DEPTH:
                        expand_biases(act, (chunk - 1) // 4, (chunk - 1) % 4)
                    if chunk == 4 * DEPTH + 1:
                        load_tokens(act)
                act.wait_ge(tokens_in, 2 * 16)
                act.wait_ge(biases, DEPTH * 4 * H * 16)
                for i in range(2):
                    act.wait_ge(written[i], 16 * ((MOD_CHUNKS + 1 - i) // 2))

            @block.vector
            def _(dve):
                dve.wait_ge(turned, 1)
                dve.tensor_copy(b.cnd[:, :, :], ps[:, 0:16].rearrange("p (c k) -> p k c", c=2)).then_inc(copied, 1)


def norm(nc, b, a, l, which, first_loads, scratch=None):
    PARTS = (0, 1, 3, 4)
    MB = len(PARTS) * KD
    with ExitStack() as ctx:
        if scratch is None:
            scratch = ctx.enter_context(sbuf(nc, "norm_scratch", [P, 2 * NT * D], F32))
        xn = scratch[:, 0:NT * D].rearrange("p (t n) -> p t n", t=NT)
        h = scratch[:, NT * D:2 * NT * D].rearrange("p (k n) -> p k n", k=KD)
        st = ctx.enter_context(sbuf(nc, "norm_stats", [P, 4, NT], F32))
        ps = ctx.enter_context(psum(nc, "ps_norm", [P, NT * 2, 512], F32))
        if which == 0:
            rows = scratch[0:3, 2 * NT * D:2 * NT * D + 4 * D]
            nrm = ctx.enter_context(sbuf(nc, "norm_rows", [16, P], F32))
            cols = ctx.enter_context(sbuf(nc, "mod_cols", [P, 3 * MB + 16], F32))
            one = ctx.enter_context(sbuf(nc, "one_plus", [P, 2, KD, 2], F32))
            pc = ctx.enter_context(psum(nc, "ps_cols", [P, 512], F32))
        with stage(nc, "squared", "dve_done", "rooted", "scaled", "turned", "h_done", "hi_done", "lo_done",
                   "mods_in", "mods_turned") as (
                squared, dve_done, rooted, scaled, turned, h_done, hi_done, lo_done, mods_in, mods_turned), nc.Block() as block:
            @block.sync
            def _(sp):
                if which == 0:
                    bias = at(l, a["b_mod"]).rearrange("(a n) -> a n", a=1)
                    for row, src in enumerate((b.mods[0:1], b.mods[1:2], bias)):
                        sp.dma_start(rows[row:row + 1, 0:2 * D], src[:, 0:2 * D]).then_inc(mods_in, 16)
                        for part in (3, 4):
                            sp.dma_start(blocks(rows[row:row + 1, (part - 1) * D:part * D]),
                                         mixed(src[:, part * D:part * D + D])).then_inc(mods_in, 16)
                    sp.dma_start(nrm[0:KD, :], at(l, a["norm1"]).rearrange("(k p) -> k p", p=P)).then_inc(mods_in, 16)
                    sp.dma_start(nrm[KD:16, :].rearrange("k (i r) -> k i r", i=4),
                                 at(l, a["norm2"]).rearrange("(i k r) -> k i r", i=4, k=KD)).then_inc(mods_in, 16)
                first_loads(sp)
                if which == 0:
                    sp.wait_ge(mods_in, 11 * 16)

            @block.scalar
            def _(act):
                for t in range(NT):
                    act.activation(xn[:, t, :], b.x[:, t, :], ACT.Square,
                                   accum_out=st[:, 0, t:t + 1]).then_inc(squared, 1)
                act.wait_ge(dve_done, 1)
                act.activation(st[:, 2, :], st[:, 1, :], ACT.Sqrt).then_inc(rooted, 1)
                for t in range(NT):
                    act.wait_ge(h_done, t + 1)
                    act.activation(b.hhi[:, :, t * P:t * P + P], h[:, :, t * P:t * P + P],
                                   ACT.Copy).then_inc(hi_done, 1)

            @block.vector
            def _(dve):
                link = Chain(dve, dve_done)
                dve.wait_ge(squared, NT)
                link(dve.tensor_scalar(st[:, 1, :], st[:, 0, :], 1.0 / D, EPS, ALU.mult, ALU.add))
                dve.wait_ge(rooted, 1)
                link(dve.reciprocal(st[:, 3, :], st[:, 2, :]))
                for t in range(NT):
                    dst, src = (blocks(xn[:, t, :]), mixed(b.x[:, t, :])) if which else (xn[:, t, :], b.x[:, t, :])
                    dve.tensor_scalar(dst, src, st[:, 3, t:t + 1], None, ALU.mult).then_inc(scaled, 1)
                if which == 0:
                    dve.wait_ge(mods_turned, 1)
                    link(dve.tensor_copy(cols[:, :], pc[:, 0:3 * MB + 16]))
                    m = cols[:, 0:3 * MB].rearrange("p (g k c) -> p g k c", g=4, k=KD)
                    for s in range(2):
                        last = dve.tensor_tensor(b.shift[:, s], m[:, 2 * s, :, 0:2],
                                                 m[:, 2 * s, :, 2:3].to_broadcast([P, KD, 2]), ALU.add)
                        last = dve.tensor_tensor(one[:, s], m[:, 2 * s + 1, :, 0:2],
                                                 m[:, 2 * s + 1, :, 2:3].to_broadcast([P, KD, 2]), ALU.add)
                    link(last)
                    link(dve.tensor_scalar(one[:, :, :, :], one[:, :, :, :], 1.0, None, ALU.add))
                    for s in range(2):
                        last = dve.tensor_tensor(
                            b.scale[:, s], one[:, s],
                            cols[:, 3 * MB + KD * s:3 * MB + KD * s + KD].unsqueeze(2).to_broadcast([P, KD, 2]),
                            ALU.mult)
                    link(last)

                def low(t):
                    dve.wait_ge(hi_done, t + 1)
                    dve.tensor_tensor(b.hlo[:, :, t * P:t * P + P], h[:, :, t * P:t * P + P],
                                      b.hhi[:, :, t * P:t * P + P].bitcast(F32), ALU.subtract).then_inc(lo_done, 1)

                for t in range(NT):
                    dve.wait_ge(turned, t + 1)
                    for k in range(KD):
                        c = min(t, 1)
                        last = dve.tensor_scalar(h[:, k, t * P:t * P + P],
                                                 ps[:, 2 * t + k // 4, (k % 4) * P:(k % 4) * P + P],
                                                 b.scale[:, which, k, c:c + 1], b.shift[:, which, k, c:c + 1],
                                                 ALU.mult, ALU.add)
                    last.then_inc(h_done, 1)
                    if t:
                        low(t - 1)
                low(NT - 1)

            @block.tensor
            def _(pe):
                if which == 0:
                    pe.wait_ge(mods_in, 11 * 16)
                    for i in range(MB):
                        pe.transpose(pc[:, 3 * i:3 * i + 3], rows[0:3, i * P:i * P + P], b.ident[0:3, 0:3])
                    pe.transpose(pc[:, 3 * MB:3 * MB + 16], nrm[:, :], b.ident[0:16, 0:16]).then_inc(mods_turned, 1)
                for t in range(NT):
                    pe.wait_ge(scaled, t + 1)
                    for k in range(KD):
                        last = pe.transpose(ps[:, 2 * t + k // 4, (k % 4) * P:(k % 4) * P + P],
                                            xn[:, t, k * P:k * P + P], b.ident)
                    last.then_inc(turned, 1)


def project_load(b, a, l, landed, sp, it, j):
    w = at(l, a["w_in"]).rearrange("(q k p) n -> q p k n", p=P, k=4)
    sp.dma_start(b.wraw[:, j, :].rearrange("p (k n) -> p k n", k=4),
                 w[j % 2][:, :, bass.ds(it * 1024 + (j // 2) * 512, 512)]).then_inc(landed[j], 16)


def project(nc, b, a, l, landed):
    N = MIX_W // 512
    with ExitStack() as ctx:
        acc = ctx.enter_context(psum(nc, "proj_acc", [P, 2 * NT, 512], F32))
        with stage(nc, "high", "split", "multiplied", "stored", "gates_in", "swapped", "scaled", "rotated",
                   also=landed) as (
                high, split, multiplied, stored, gates_in, swapped, scaled, rotated), nc.Block() as block:
            scratch = b.y[:, :, :, :].rearrange("p t b n -> p (t b n)")
            bias = scratch[:, 0:2 * D].rearrange("p (g n) -> p g n", g=2)

            @block.sync
            def _(sp):
                for g in range(2):
                    part = slice((2 + 3 * g) * D, (3 + 3 * g) * D)
                    sp.dma_start(bias[:, g, :], at(l, a["b_mod"])[part].partition_broadcast(P)).then_inc(gates_in, 16)
                    for c in range(2):
                        sp.dma_start(b.gate[g][:, c, :], b.mods[c, part].partition_broadcast(P)).then_inc(gates_in, 16)
                with sp.Fori(1, N // 2) as it:
                    for j in range(4):
                        sp.wait_ge(split, it * 4 + (j + 1))
                        project_load(b, a, l, landed, sp, it, j)

            @block.gpsimd
            def _(pool):
                pool.wait_ge(gates_in, 6 * 16)
                for g in range(2):
                    pool.tensor_tensor(b.gate[g][:, :, :], b.gate[g][:, :, :],
                                       bias[:, g, :].unsqueeze(1).to_broadcast([P, 2, D]), ALU.add).then_inc(rotated, 1)
                pool.wait_ge(rotated, 2)
                swap = scratch[:, 0:2 * 1536].rearrange("p (t n) -> p t n", t=2)
                for c, n, o, chunks in ((QA, 1024, 0, 2), (QB, 512, 1024, 4)):
                    pool.wait_ge(stored, 2 + chunks)
                    for t in range(2):
                        x = b.proj[:, 1 + t, c:c + n].rearrange("p (g a j d) -> p g a j d", a=2, j=2, d=16)
                        s = swap[:, t, o:o + n].rearrange("p (g a j d) -> p g a j d", a=2, j=2, d=16)
                        sin = b.cst[:, C_SIN + 64 * t:C_SIN + 64 * t + 64].rearrange("p (a j d) -> p a j d", a=2, j=2)
                        for j in range(2):
                            pool.tensor_tensor(s[:, :, :, j, :], x[:, :, :, 1 - j, :],
                                               sin[:, :, j, :].unsqueeze(1).to_broadcast([P, n // 64, 2, 16]),
                                               ALU.mult).then_inc(swapped, 1)
                    pool.wait_ge(swapped, 2 * chunks)
                    for t in range(2):
                        x = b.proj[:, 1 + t, c:c + n].rearrange("p (g d) -> p g d", d=64)
                        cos = b.cst[:, C_COS + 64 * t:C_COS + 64 * t + 64]
                        pool.tensor_tensor(x, x, cos.unsqueeze(1).to_broadcast([P, n // 64, 64]),
                                           ALU.mult).then_inc(scaled, 1)
                    pool.wait_ge(scaled, chunks)
                    for t in range(2):
                        x = b.proj[:, 1 + t, c:c + n]
                        pool.tensor_tensor(x, x, swap[:, t, o:o + n], ALU.add).then_inc(rotated, 1)
                pool.wait_ge(rotated, 6)

            @block.scalar
            def _(act):
                with act.Fori(0, N // 2) as it:
                    for j in range(4):
                        high_unit(act, b, landed, multiplied, high, it * 4, j)

            @block.vector
            def _(dve):
                dve.sem_inc(split, RAW)
                dve.sem_inc(stored, 2)

                def store(chunk, half):
                    dve.wait_ge(multiplied, chunk * 2 + (SPL + 2))
                    dve.tensor_scalar(b.proj[:, :, bass.ds(chunk * 512, 512)],
                                      acc[:, NT * half:NT * half + NT, :], 1.0, None, ALU.mult).then_inc(stored, 1)

                def body(it, last):
                    low_unit(dve, b, high, split, it * 4, 1)
                    low_unit(dve, b, high, split, it * 4, 2)
                    store(it * 2, 0)
                    low_unit(dve, b, high, split, it * 4, 3)
                    if not last:
                        low_unit(dve, b, high, split, it * 4, 4)
                    store(it * 2 + 1, 1)

                low_unit(dve, b, high, split, 0, 0)
                with dve.Fori(0, N // 2 - 1) as it:
                    body(it, False)
                body(N // 2 - 1, True)

            @block.tensor
            def _(pe):
                pe.sem_inc(multiplied, SPL)
                with pe.Fori(0, N // 2) as it:
                    for j in range(4):
                        half = j // 2
                        if j % 2 == 0:
                            pe.wait_ge(stored, it * 2 + (half + 1))
                        pe.wait_ge(split, it * 4 + (j + 1 + RAW))
                        for k4 in range(4):
                            k = 4 * (j % 2) + k4
                            c = slice(k4 * 512, k4 * 512 + 512)
                            for t in range(NT):
                                r = slice(t * P, t * P + P)
                                last = product(pe, acc[:, NT * half + t, :], b.hhi[:, k, r], b.hlo[:, k, r],
                                               b.whi[:, j % SPL, c], b.wlo[:, j % SPL, c], k == 0, k == KD - 1)
                        last.then_inc(multiplied, 1)


def turn_heads(pe, b, tp, turns, turned, turns_copied):
    for n in range(len(turns) // 4):
        if n >= 2:
            pe.wait_ge(turns_copied, n - 1)
        for i in range(4):
            last = pe.transpose(tp[:, n % 2, i * P:i * P + P], turns[4 * n + i], b.ident)
        last.then_inc(turned, 1)


def copy_turns(act, tp, heads, count, turned, turns_copied):
    for n in range(count // 4):
        act.wait_ge(turned, n + 1)
        act.activation(heads[:, 4 * n:4 * n + 4, :].rearrange("p a t -> p (a t)"), tp[:, n % 2, :],
                       ACT.Copy).then_inc(turns_copied, 1)


def attention(nc, b, a, l):
    DF, NA = 0, 1
    Q0, K0, V0 = (QA, QC), (KA, KC), (VA, VC)
    DQ = (DH // 2, DH)
    SCALE = [float(d) ** -0.5 for d in DQ]
    units = [(t, h) for t in range(NT) for h in range(H)]
    U = len(units)
    GROUPS = 7 * H // 4
    with ExitStack() as ctx:
        sb = lambda n, s: ctx.enter_context(sbuf(nc, n, s, F32))
        ps = lambda n, s: ctx.enter_context(psum(nc, n, s, F32))
        heads = [sb(n, [P, 7 * H, P]) for n in ("diff_heads", "na_heads")]
        qt = [x[:, 0:NT * H, :].rearrange("p (h t) n -> p h t n", h=H) for x in heads]
        kt = [x[:, NT * H:7 * H, :].rearrange("p (h s) n -> p h (s n)", h=H) for x in heads]
        kc = sb("cache_k", [P, 2, H, DH])
        vc = sb("cache_v", [P, 2, H, DH])
        prd = sb("diff_probs", [P, 2, 2, 384])
        prn = sb("na_probs", [P, 2, 384])
        pt = sb("probs_t", [P, 2, 384])
        st = sb("softmax_stats", [P, 7, U, 2])
        mx, nm, sm, rc, r2, smn, rcn = (st[:, i] for i in range(7))
        lq = sb("lambda_in", [P, 4, 64])
        lt = sb("lambda_work", [P, 2, 64])
        lw = sb("lambda_vals", [P, 8])
        gn = sb("diff_gain", [P, DH])
        sq = sb("squares", [P, DH])
        hs = sb("head_stats", [P, 4, U])
        dec = sb("ret_decay", [P, 8])
        lgw = sb("log_work", [P, 6, 8])
        mxn = sb("na_maxima", [P, 2, U])
        bias = sb("na_bias", [P, 2, H, LAT])
        sc = sb("na_scores", [P, 2, 384])
        sd = ps("ps_diff_scores", [P, 2, 2, 512])
        sn = ps("ps_na_scores", [P, 512])
        p2 = ps("ps_probs", [P, 2, 512])
        po = ps("ps_out", [P, 512])

        def keys(t):
            return (0, 1) if t == 0 else (1, 3)

        width = [keys(t)[1] * P for t, h in units]

        with stage(nc, "diff_loaded", "na_loaded", "written", "turned", "turns_copied", "scored_d", "scored_n",
                   "dve_done", "shifted_d", "shifted_n", "expd_d", "expd_n", "weighed", "p_turned_d", "p_turned_n",
                   "p_copied_d", "p_copied_n", "o_done", "o_copied", "lam_sum", "lam_exp", "rooted", "biased",
                   "squared", "decay_in", "decay_exp") as (
                diff_loaded, na_loaded, written, turned, turns_copied, scored_d, scored_n, dve_done, shifted_d,
                shifted_n, expd_d, expd_n, weighed, p_turned_d, p_turned_n, p_copied_d, p_copied_n, o_done, o_copied,
                lam_sum, lam_exp, rooted, biased, squared, decay_in, decay_exp), nc.Block() as block:
            p_turned, p_copied = (p_turned_d, p_turned_n), (p_copied_d, p_copied_n)

            def head_out(u):
                t, h = units[u]
                return b.y[:, t, 0, h * DH:h * DH + DH]

            @block.sync
            def _(sp):
                for i, (ck, cv, loaded) in enumerate((("cache_diff_k", "cache_diff_v", diff_loaded),
                                                      ("cache_na_k", "cache_na_v", na_loaded))):
                    sp.dma_start(kc[:, i], at(l, a[ck][0]).rearrange("h s d -> s h d")).then_inc(loaded, 16)
                    sp.dma_start(vc[:, i], at(l, a[cv][0]).rearrange("h s d -> s h d")).then_inc(loaded, 16)
                    if i == DF:
                        sp.dma_start(lq[:, :, :], at(l, a["diff_lambda"]).partition_broadcast(P)).then_inc(loaded, 16)
                        sp.dma_start(gn[:, :], at(l, a["diff_gn"]).partition_broadcast(P)).then_inc(loaded, 16)
                        sp.dma_start(dec[:, :], at(l, a["ret_decay"]).rearrange("d h -> (d h)")
                                     .partition_broadcast(P)).then_inc(decay_in, 16)
                    else:
                        sp.dma_start(bias[:, :, :, :], at(l, b.bias)).then_inc(loaded, 16)
                for out, col in (("o_diff_k", KA), ("o_diff_v", VA), ("o_na_k", KC), ("o_na_v", VC)):
                    sp.dma_start(at(l, a[out][0]).rearrange("h s d -> s h d"),
                                 b.proj[:, 0, col:col + 512].rearrange("p (h d) -> p h d", h=H)).then_inc(written, 16)
                sp.wait_ge(written, 64)

            @block.scalar
            def _(act):
                for n in range(2 * GROUPS):
                    act.wait_ge(turned, n + 1)
                    act.activation(heads[n // GROUPS][:, 4 * (n % GROUPS):4 * (n % GROUPS) + 4, :]
                                   .rearrange("p a t -> p (a t)"), p2[:, n % 2, :], ACT.Copy).then_inc(turns_copied, 1)
                    if n == GROUPS - 1:
                        act.wait_ge(lam_sum, 1)
                        act.activation(lw[:, 2:4], lw[:, 0:2], ACT.Exp).then_inc(lam_exp, 1)
                        act.wait_ge(decay_in, 16)
                        act.activation(lgw[:, 0, :], dec[:, :], ACT.Abs).then_inc(decay_exp, 1)
                        act.wait_ge(decay_exp, 1)
                        act.activation(lgw[:, 1, :], lgw[:, 0, :], ACT.Exp, scale=-1.0).then_inc(decay_exp, 1)

                def diff_exps(u):
                    act.wait_ge(shifted_d, u + 1)
                    if u >= 2:
                        act.wait_ge(p_turned_d, u - 1)
                    for i in range(2):
                        act.activation(prd[:, u % 2, i, 0:width[u]], sd[:, u % 2, i, 0:width[u]], ACT.Exp,
                                       bias=nm[:, u, i:i + 1], scale=SCALE[DF],
                                       accum_out=sm[:, u, i:i + 1]).then_inc(expd_d, 1)

                def na_exp(u):
                    act.wait_ge(shifted_n, u + 1)
                    if u >= 2:
                        act.wait_ge(p_turned_n, u - 1)
                    act.activation(prn[:, u % 2, 0:width[u]], sc[:, u % 2, 0:width[u]], ACT.Exp,
                                   bias=mxn[:, 1, u:u + 1], accum_out=smn[:, u, 0:1]).then_inc(expd_n, 1)

                def probs_out(u, kind):
                    act.wait_ge(p_turned[kind], u + 1)
                    if u >= 1:
                        act.wait_ge(o_done, 2 * u - 1 + kind)
                    act.activation(pt[:, kind, 0:width[u]], p2[:, kind, 0:width[u]], ACT.Copy)\
                        .then_inc(p_copied[kind], 1)

                def square(u):
                    act.wait_ge(o_copied, 2 * u + 1)
                    if u >= 1:
                        act.wait_ge(squared, u)
                    act.activation(sq[:, :], head_out(u), ACT.Square, accum_out=hs[:, 0, u:u + 1]).then_inc(squared, 1)

                diff_exps(0)
                na_exp(0)
                for u in range(U):
                    probs_out(u, DF)
                    if u + 1 < U:
                        diff_exps(u + 1)
                    probs_out(u, NA)
                    if u + 1 < U:
                        na_exp(u + 1)
                    if u >= 1:
                        square(u - 1)
                square(U - 1)
                act.wait_ge(rooted, 1)
                act.activation(hs[:, 2, :], hs[:, 1, :], ACT.Sqrt).then_inc(rooted, 1)

            @block.vector
            def _(dve):
                link = Chain(dve, dve_done)
                dve.wait_ge(diff_loaded, 64)
                link(dve.tensor_copy(lw[:, 4:6], b.cst[:, bass.ds(C_LAM + 2 * l, 2)]))
                link(dve.tensor_tensor(lt[:, :, :], lq[:, 0::2, :], lq[:, 1::2, :], ALU.mult))
                dve.tensor_reduce(lw[:, 0:2], lt[:, :, :], AX_X, ALU.add).then_inc(lam_sum, 1)
                dve.wait_ge(na_loaded, 48)
                link(dve.tensor_tensor(
                    bias[:, :, :, :].rearrange("p a h (j n) -> p (a h j) n", j=4),
                    bias[:, :, :, :].rearrange("p a h (j n) -> p (a h j) n", j=4),
                    b.cst[:, C_NM:C_NM + 64].unsqueeze(1).to_broadcast([P, 32, 64]), ALU.add))
                dve.wait_ge(lam_exp, 1)
                link(dve.tensor_tensor(lw[:, 6:7], lw[:, 3:4], lw[:, 2:3], ALU.subtract))
                link(dve.tensor_tensor(lw[:, 7:8], lw[:, 6:7], lw[:, 4:5], ALU.subtract))
                link(dve.tensor_scalar(gn[:, :], gn[:, :], lw[:, 5:6], None, ALU.mult))

                dve.wait_ge(decay_exp, 2)
                e, z, z2, q, w = (lgw[:, i, :] for i in (1, 2, 3, 4, 5))
                link(dve.tensor_scalar(z, e, 2.0, None, ALU.add))
                link(dve.reciprocal(z2, z))
                link(dve.tensor_tensor(z, e, z2, ALU.mult))
                link(dve.tensor_tensor(z2, z, z, ALU.mult))
                link(dve.tensor_scalar(q, z2, 2.0 / 17, 2.0 / 15, ALU.mult, ALU.add))
                for n in (13, 11, 9, 7, 5, 3, 1):
                    link(dve.tensor_tensor(w, q, z2, ALU.mult))
                    link(dve.tensor_scalar(q, w, 2.0 / n, None, ALU.add))
                link(dve.tensor_tensor(w, q, z, ALU.mult))
                link(dve.tensor_scalar(q, dec[:, :], 0.0, None, ALU.min))
                link(dve.tensor_tensor(b.lg[:, :], q, w, ALU.subtract))
                pairs = b.lg[:, :].rearrange("p (d r h) -> p d r h", d=2, h=2)
                dve.tensor_copy(b.lgp[0:64], pairs[0:64, :, :, 0])
                dve.tensor_copy(b.lgp[64:128], pairs[64:128, :, :, 1])

                def diff_maxima(u):
                    dve.wait_ge(scored_d, u + 1)
                    link(dve.tensor_reduce(mx[:, u, :], sd[:, u % 2, :, 0:width[u]], AX_X, ALU.max))
                    dve.tensor_scalar(nm[:, u, :], mx[:, u, :], -SCALE[DF], None, ALU.mult).then_inc(shifted_d, 1)

                def na_maxima(u):
                    t, h = units[u]
                    dve.wait_ge(scored_n, u + 1)
                    if u >= 2:
                        dve.wait_ge(expd_n, u - 1)
                    if t == 0:
                        link(dve.tensor_scalar(sc[:, u % 2, 0:P], sn[:, 0:P], SCALE[NA], None, ALU.mult))
                    else:
                        dve.tensor_scalar(sc[:, u % 2, 0:P], sn[:, 0:P], SCALE[NA], None, ALU.mult).then_inc(biased, 1)
                        link(dve.scalar_tensor_tensor(sc[:, u % 2, P:3 * P], sn[:, P:3 * P], SCALE[NA],
                                                      bias[:, t - 1, h, :], ALU.mult, ALU.add))
                        dve.wait_ge(biased, u + 1 - H)
                    link(dve.tensor_reduce(mxn[:, 0, u:u + 1], sc[:, u % 2, 0:width[u]], AX_X, ALU.max))
                    dve.tensor_scalar(mxn[:, 1, u:u + 1], mxn[:, 0, u:u + 1], -1.0, None, ALU.mult)\
                        .then_inc(shifted_n, 1)

                def weigh(u):
                    dve.wait_ge(expd_d, 2 * (u + 1))
                    link(dve.reciprocal(rc[:, u, :], sm[:, u, :]))
                    p = prd[:, u % 2]
                    dve.tensor_scalar(r2[:, u, 1:2], rc[:, u, 1:2], lw[:, 7:8], None, ALU.mult)
                    link(dve.tensor_scalar(p[:, 0, 0:width[u]], p[:, 0, 0:width[u]], rc[:, u, 0:1], None, ALU.mult))
                    dve.scalar_tensor_tensor(p[:, 0, 0:width[u]], p[:, 1, 0:width[u]], r2[:, u, 1:2],
                                             p[:, 0, 0:width[u]], ALU.mult, ALU.add).then_inc(weighed, 1)

                def diff_out(u):
                    dve.wait_ge(o_done, 2 * u + 1)
                    dve.tensor_copy(head_out(u), po[:, 0:DH]).then_inc(o_copied, 1)

                def na_out(u):
                    t, h = units[u]
                    dve.wait_ge(expd_n, u + 1)
                    link(dve.reciprocal(rcn[:, u, 0:1], smn[:, u, 0:1]))
                    dve.wait_ge(o_done, 2 * u + 2)
                    dve.tensor_scalar(b.y[:, t, 2, h * DH:h * DH + DH], po[:, 0:DH], rcn[:, u, 0:1], None,
                                      ALU.mult).then_inc(o_copied, 1)

                diff_maxima(0)
                na_maxima(0)
                for u in range(U):
                    weigh(u)
                    if u >= 1:
                        na_out(u - 1)
                    if u + 1 < U:
                        diff_maxima(u + 1)
                    if u + 1 < U:
                        na_maxima(u + 1)
                    diff_out(u)
                na_out(U - 1)
                dve.wait_ge(squared, U)
                dve.tensor_scalar(hs[:, 1, :], hs[:, 0, :], 1.0 / DH, EPS, ALU.mult, ALU.add).then_inc(rooted, 1)
                dve.wait_ge(rooted, 2)
                link(dve.reciprocal(hs[:, 3, :], hs[:, 2, :]))
                y = b.y[:, :, 0, :].rearrange("p t (h d) -> p t h d", h=H)
                link(dve.tensor_tensor(y, y, hs[:, 3, :].rearrange("p (t h) -> p t h", h=H).unsqueeze(3)
                                       .to_broadcast([P, NT, H, DH]), ALU.mult))
                link(dve.tensor_tensor(y, y, gn[:, :].unsqueeze(1).unsqueeze(1).to_broadcast([P, NT, H, DH]), ALU.mult))

            @block.tensor
            def _(pe):
                def turn_heads(kind):
                    turns = [b.proj[:, t, Q0[kind] + h * DH:Q0[kind] + h * DH + DH] for h in range(H)
                             for t in range(NT)]
                    for h in range(H):
                        own = [b.proj[:, t, K0[kind] + h * DH:K0[kind] + h * DH + DH] for t in range(NT)]
                        turns += [own[0], kc[:, kind, h, :], own[1], own[2]]
                    for g in range(GROUPS):
                        n = GROUPS * kind + g
                        if g == NT:
                            pe.wait_ge((diff_loaded, na_loaded)[kind], (64, 48)[kind])
                        if n >= 2:
                            pe.wait_ge(turns_copied, n - 1)
                        for i in range(4):
                            last = pe.transpose(p2[:, n % 2, i * P:i * P + P], turns[4 * g + i], b.ident)
                        last.then_inc(turned, 1)

                def diff_scores(u):
                    t, h = units[u]
                    f, n = keys(t)
                    if u >= 2:
                        pe.wait_ge(expd_d, 2 * (u - 1))
                    for i in range(2):
                        r = slice(64 * i, 64 * i + 64)
                        last = pe.matmul(sd[:, u % 2, i, 0:n * P], qt[DF][r, h, t, :], kt[DF][r, h, f * P:(f + n) * P],
                                         start=True, stop=True, skip_group_check=True)
                    last.then_inc(scored_d, 1)

                def na_scores(u):
                    t, h = units[u]
                    f, n = keys(t)
                    if u >= 1:
                        pe.wait_ge(shifted_n, u)
                    pe.matmul(sn[:, 0:n * P], qt[NA][:, h, t, :], kt[NA][:, h, f * P:(f + n) * P], start=True,
                              stop=True, skip_group_check=True).then_inc(scored_n, 1)

                def turn_probs(u, kind):
                    if kind == DF:
                        pe.wait_ge(weighed, u + 1)
                        src = prd[:, u % 2, 0]
                    else:
                        pe.wait_ge(expd_n, u + 1)
                        src = prn[:, u % 2]
                    if u >= 1:
                        pe.wait_ge(p_copied[kind], u)
                    for i in range(width[u] // P):
                        last = pe.transpose(p2[:, kind, i * P:i * P + P], src[:, i * P:i * P + P], b.ident)
                    last.then_inc(p_turned[kind], 1)

                def values(u, kind):
                    t, h = units[u]
                    v = [b.proj[:, i, V0[kind] + h * DH:V0[kind] + h * DH + DH] for i in range(NT)]
                    v = [v[0]] if t == 0 else [vc[:, kind, h, :], v[1], v[2]]
                    pe.wait_ge(p_copied[kind], u + 1)
                    if 2 * u + kind:
                        pe.wait_ge(o_copied, 2 * u + kind)
                    for i, vi in enumerate(v):
                        last = pe.matmul(po[:, 0:DH], pt[:, kind, i * P:i * P + P], vi,
                                         start=(i == 0), stop=(i == len(v) - 1), skip_group_check=True)
                    last.then_inc(o_done, 1)

                turn_heads(DF)
                pe.wait_ge(turns_copied, GROUPS)
                diff_scores(0)
                turn_heads(NA)
                pe.wait_ge(turns_copied, 2 * GROUPS)
                na_scores(0)
                for u in range(U):
                    if u + 1 < U:
                        diff_scores(u + 1)
                    if u >= 1:
                        values(u - 1, NA)
                    turn_probs(u, DF)
                    if u + 1 < U:
                        na_scores(u + 1)
                    turn_probs(u, NA)
                    values(u, DF)
                values(U - 1, NA)


def retention(nc, b, a, l):
    PR = H // 2
    with ExitStack() as ctx:
        sb = lambda n, s: ctx.enter_context(sbuf(nc, n, s, F32))
        ps = lambda n, s: ctx.enter_context(psum(nc, n, s, F32))
        heads = sb("ret_heads", [P, 12, P])
        gn = sb("ret_gain", [P, DH])
        s0 = sb("ret_state", [P, 2, PR, DH])
        dm = sb("decay_mats", [P, 2, H, 2, P])
        qd = sb("q_decay", [P, 2, PR, LAT])
        ke = sb("k_decay", [P, 2, H])
        kd = sb("k_decayed", [P, H, 2, 64])
        sa = sb("decayed_scores", [P, 2, 2, 4, P])
        og = sb("ret_out", [P, 2, 2, NT, DH])
        sq = sb("ret_squares", [P, 2, DH])
        hs = sb("ret_stats", [P, 3, H, 2 * NT])
        so = sb("state_out", [64, 2, H, DH])
        s = ps("ps_scores", [P, 2, 2, 512])
        po = ps("ps_out", [P, 2, 512])
        pst = ps("ps_state", [64, 2, 512])
        qt = heads[:, 0:6, :].rearrange("p (r t) n -> p r (t n)", r=PR)
        kt = heads[:, 6:12, :].rearrange("p (r t) n -> p r (t n)", r=PR)
        with stage(nc, "loaded", "written", "turned", "turns_copied", "scored", "dve_done", "mats", "ends",
                   "masked", "s_decayed", "o_done", "o_copied", "k_scaled", "states", "s_out", "edges", "q_ready",
                   "squared", "rooted", "silu_done", "gate_ready") as (
                loaded, written, turned, turns_copied, scored, dve_done, mats, ends, masked, s_decayed, o_done,
                o_copied, k_scaled, states, s_out, edges, q_ready, squared, rooted, silu_done,
                gate_ready), nc.Block() as block:
            @block.sync
            def _(sp):
                sp.dma_start(gn[:, :], at(l, a["ret_gn"]).partition_broadcast(P)).then_inc(loaded, 16)
                for d in range(2):
                    sp.dma_start(s0[:, d, :, :], at(l, a["state_ret"][0])[d].rearrange("(r h) k v -> (h k) r v", h=2))\
                        .then_inc(loaded, 16)
                sp.wait_ge(s_out, 2)
                for d in range(2):
                    sp.dma_start(at(l, a["o_state"][0])[d].rearrange("h k v -> k h v"), so[:, d, :, :])\
                        .then_inc(written, 16)
                sp.wait_ge(written, 32)

            @block.scalar
            def _(act):
                for d in range(2):
                    for h in range(H):
                        i = d * H + h
                        act.activation(dm[:, d, h, :, :].rearrange("p a t -> p (a t)"),
                                       b.cst[:, C_D0 + 256 * d:C_D0 + 256 * d + 256], ACT.Exp,
                                       scale=b.lg[:, i:i + 1]).then_inc(mats, 1)
                    if d == 0:
                        copy_turns(act, po, heads, 12, turned, turns_copied)
                for d in range(2):
                    for r in range(PR):
                        act.activation(qd[:, d, r, :], b.cst[:, C_QE + 256 * d:C_QE + 256 * d + 256], ACT.Exp,
                                       scale=b.lgp[:, d, r:r + 1]).then_inc(edges, 1)
                for d in range(2):
                    for h in range(H):
                        i = d * H + h
                        act.activation(ke[:, d, h:h + 1], b.cst[:, C_KE + d:C_KE + d + 1], ACT.Exp,
                                       scale=b.lg[:, i:i + 1]).then_inc(ends, 1)
                act.activation(b.proj[:, :, GB:GB + 1024], b.proj[:, :, GB:GB + 1024], ACT.Silu)\
                    .then_inc(silu_done, 1)
                for h in range(H):
                    act.wait_ge(o_copied, h + 1)
                    for i in range(2 * NT):
                        n = h * 2 * NT + i
                        if n >= 2:
                            act.wait_ge(squared, n - 1)
                        act.activation(sq[:, n % 2, :], og[:, h % 2, i // NT, i % NT, :], ACT.Square,
                                       accum_out=hs[:, 0, h, i:i + 1]).then_inc(squared, 1)
                    act.wait_ge(squared, 2 * NT * (h + 1))
                    act.activation(hs[:, 1, h, :], hs[:, 0, h, :], ACT.Sqrt, scale=1.0 / DH,
                                   bias=b.cst[:, C_EPS:C_EPS + 1]).then_inc(rooted, 1)

            @block.gpsimd
            def _(pool):
                pool.wait_ge(edges, 4)
                pool.wait_ge(turns_copied, 3)
                for d in range(2):
                    pool.tensor_tensor(qd[:, d], qd[:, d], qt[:, :, P:3 * P], ALU.mult).then_inc(q_ready, 1)
                pool.wait_ge(ends, 8)
                pool.tensor_scalar(ke[:, :, :], ke[:, :, :], 0.125, None, ALU.mult).then_inc(k_scaled, 1)
                pool.wait_ge(k_scaled, 1)
                for d in range(2):
                    pool.tensor_tensor(kd[:, :, d, :], b.proj[:, 0, KB:KB + 64 * H].rearrange("p (h k) -> p h k", h=H),
                                       ke[:, d, :].unsqueeze(2).to_broadcast([P, H, 64]), ALU.mult)\
                        .then_inc(k_scaled, 1)
                pool.wait_ge(loaded, 48)
                pool.wait_ge(silu_done, 1)
                for h in range(H):
                    for d in range(2):
                        c = GB + 512 * d + DH * h
                        pool.tensor_tensor(b.proj[:, :, c:c + DH], b.proj[:, :, c:c + DH],
                                           gn[:, :].unsqueeze(1).to_broadcast([P, NT, DH]), ALU.mult)\
                            .then_inc(gate_ready, 1)

            @block.vector
            def _(dve):
                link = Chain(dve, dve_done)
                for d in range(2):
                    dve.wait_ge(mats, H * (d + 1))
                    m = b.cst[:, C_M0 + 128 * d:C_M0 + 128 * d + 128]
                    dve.scalar_tensor_tensor(dm[:, d, :, 0, :], dm[:, d, :, 0, :], 0.125,
                                             m.unsqueeze(1).to_broadcast([P, H, P]), ALU.mult, ALU.mult)\
                        .then_inc(masked, 1)
                    dve.tensor_scalar(dm[:, d, :, 1, :], dm[:, d, :, 1, :], 0.125, None, ALU.mult).then_inc(masked, 1)
                dve.wait_ge(masked, 4)

                def decay(h):
                    dve.wait_ge(scored, h + 1)
                    if h >= 2:
                        dve.wait_ge(o_done, h - 1)
                    sh = s[:, h % 2]
                    sf, sbk = sa[:, h % 2, 0], sa[:, h % 2, 1]
                    f, k = dm[:, 0, h], dm[:, 1, h]
                    dve.tensor_tensor(sf[:, 0, :], sh[:, 0, 0:128], f[:, 0, :], ALU.mult).then_inc(s_decayed, 1)
                    dve.tensor_tensor(sf[:, 1:3, :], sh[:, 0, 128:384].rearrange("p (a t) -> p a t", a=2), f,
                                      ALU.mult).then_inc(s_decayed, 1)
                    dve.tensor_tensor(sf[:, 3, :], sh[:, 1, 128:256], f[:, 0, :], ALU.mult).then_inc(s_decayed, 1)
                    dve.tensor_tensor(sbk[:, 0:2, :], sh[:, 0, 0:256].rearrange("p (a t) -> p a t", a=2),
                                      k[:, 0, :].unsqueeze(1).to_broadcast([P, 2, P]), ALU.mult)\
                        .then_inc(s_decayed, 1)
                    dve.tensor_tensor(sbk[:, 2, :], sh[:, 1, 0:128], k[:, 1, :], ALU.mult).then_inc(s_decayed, 1)
                    dve.tensor_tensor(sbk[:, 3, :], sh[:, 1, 128:256], k[:, 0, :], ALU.mult).then_inc(s_decayed, 1)

                def copy_out(h):
                    dve.wait_ge(o_done, h + 1)
                    dve.tensor_copy(og[:, h % 2], po[:, :, 0:NT * P].rearrange("p d (t n) -> p d t n", t=NT))\
                        .then_inc(o_copied, 1)

                def finish(h):
                    dve.wait_ge(rooted, h + 1)
                    link(dve.reciprocal(hs[:, 2, h, :], hs[:, 1, h, :]))
                    flat = og[:, h % 2].rearrange("p d t v -> p (d t) v")
                    link(dve.tensor_tensor(flat, flat, hs[:, 2, h, :].unsqueeze(2).to_broadcast([P, 2 * NT, DH]),
                                           ALU.mult))
                    dve.wait_ge(gate_ready, 2 * h + 2)
                    for d in range(2):
                        c = GB + 512 * d + DH * h
                        last = dve.tensor_tensor(og[:, h % 2, d], og[:, h % 2, d], b.proj[:, :, c:c + DH], ALU.mult)
                    link(last)
                    link(dve.tensor_tensor(b.y[:, :, 1, h * DH:h * DH + DH], og[:, h % 2, 0], og[:, h % 2, 1], ALU.add))

                decay(0)
                for h in range(H):
                    if h + 1 < H:
                        decay(h + 1)
                    copy_out(h)
                    if h == 2:
                        dve.wait_ge(states, 1)
                        for d in range(2):
                            dve.tensor_copy(so[:, d, :, :], pst[:, d, :].rearrange("p (h v) -> p h v", h=H))\
                                .then_inc(s_out, 1)
                    if h >= 1:
                        finish(h - 1)
                finish(H - 1)

            @block.tensor
            def _(pe):
                turns = [b.proj[:, t, c + r * P:c + r * P + P] for c in (QB, KB) for r in range(PR) for t in range(NT)]
                turn_heads(pe, b, po, turns, turned, turns_copied)
                pe.wait_ge(turns_copied, 3)

                def score(h):
                    r, rows = h // 2, slice(64 * (h % 2), 64 * (h % 2) + 64)
                    sh = s[:, h % 2]
                    if h >= 2:
                        pe.wait_ge(s_decayed, 6 * (h - 1))
                    pe.matmul(sh[:, 0, 0:P], kt[rows, r, 0:P], qt[rows, r, 0:P], start=True, stop=True,
                              skip_group_check=True)
                    pe.matmul(sh[:, 0, P:3 * P], kt[rows, r, P:2 * P], qt[rows, r, P:3 * P], start=True, stop=True,
                              skip_group_check=True)
                    pe.matmul(sh[:, 1, 0:2 * P], kt[rows, r, 2 * P:3 * P], qt[rows, r, P:3 * P], start=True,
                              stop=True, skip_group_check=True).then_inc(scored, 1)

                def add(h):
                    r, rows = h // 2, slice(64 * (h % 2), 64 * (h % 2) + 64)
                    v = [b.proj[:, t, VB + h * DH:VB + h * DH + DH] for t in range(NT)]
                    pe.wait_ge(s_decayed, 6 * h + 6)
                    if h == 0:
                        pe.wait_ge(q_ready, 2)
                        pe.wait_ge(loaded, 48)
                    else:
                        pe.wait_ge(o_copied, h)
                    terms = {(0, 0): [(0, 0)], (0, 1): [(1, 1)], (0, 2): [(2, 1), (3, 2)],
                             (1, 0): [(0, 0)], (1, 1): [(1, 1), (2, 2)], (1, 2): [(3, 2)]}
                    for (d, t), blks in terms.items():
                        out = po[:, d, t * P:t * P + P]
                        for i, (blk, vt) in enumerate(blks):
                            last = pe.matmul(out, sa[:, h % 2, d, blk, :], v[vt], start=(i == 0),
                                             stop=(t == 0 and i == len(blks) - 1), skip_group_check=True)
                        if t:
                            last = pe.matmul(out, qd[rows, d, r, (t - 1) * P:t * P], s0[rows, d, r, :], start=False,
                                             stop=True, skip_group_check=True)
                    last.then_inc(o_done, 1)

                score(0)
                score(1)
                for h in range(H):
                    if h == 1:
                        pe.wait_ge(k_scaled, 3)
                        for d in range(2):
                            for g in range(H):
                                last = pe.matmul(pst[:, d, g * DH:g * DH + DH], kd[:, g, d, :],
                                                 b.proj[:, 0, VB + g * DH:VB + g * DH + DH], start=True, stop=True,
                                                 skip_group_check=True)
                        last.then_inc(states, 1)
                    add(h)
                    if h + 2 < H:
                        score(h + 2)



def turn_blocks(pe, b, tp, src, count, turned, lo_done):
    for n in range(count):
        if n >= 2:
            pe.wait_ge(lo_done, n - 1)
        for t in range(NT):
            last = pe.transpose(tp[:, n % 2, t * P:t * P + P], src(t, n), b.ident)
        last.then_inc(turned, 1)


def high_blocks(act, tp, hi, count, turned, hi_done):
    for n in range(count):
        act.wait_ge(turned, n + 1)
        act.activation(hi[:, n, :], tp[:, n % 2, 0:TOK], ACT.Copy).then_inc(hi_done, 1)


def low_blocks(dve, tp, hi, lo, count, hi_done, lo_done):
    for n in range(count):
        dve.wait_ge(hi_done, n + 1)
        dve.tensor_tensor(lo[:, n, :], tp[:, n % 2, 0:TOK], hi[:, n, :].bitcast(F32),
                          ALU.subtract).then_inc(lo_done, 1)


def merge(nc, b, a, l):
    w = at(l, a["w_in"]).rearrange("(q k p) n -> q p k n", p=P, k=4)
    wb = at(l, a["w_branch"])
    R3 = 3
    with ExitStack() as ctx:
        yhi = ctx.enter_context(sbuf(nc, "y_hi", [P, NB * 4, TOK], F32R))
        ylo = ctx.enter_context(sbuf(nc, "y_lo", [P, NB * 4, TOK], F32R))
        sg = ctx.enter_context(sbuf(nc, "merge_gate", [P, NT, 512], F32))
        tp = ctx.enter_context(psum(nc, "ps_y", [P, 2, 512], F32))
        acc = ctx.enter_context(psum(nc, "merge_acc", [P, 2 * NT, 512], F32))
        units = NB * 2 * R3
        with stage(nc, *[f"landed{j}" for j in range(3)], "high", "split", "multiplied", "gated", "joined",
                   "merged", "turned", "hi_done", "lo_done") as (
                *landed, high, split, multiplied, gated, joined, merged, turned, hi_done, lo_done), nc.Block() as block:
            @block.sync
            def _(sp):
                for br in range(NB):
                    for cc in range(2):
                        for j in range(R3):
                            n = (br * 2 + cc) * R3 + j
                            if n >= 3:
                                sp.wait_ge(split, n - 2)
                            if j < 2:
                                c = MG + br * D + cc * 512
                                src = w[j][:, :, c:c + 512]
                            else:
                                src = wb[br].rearrange("(k p) n -> p k n", p=P)[:, :, cc * 512:cc * 512 + 512]
                            sp.dma_start(b.wraw[:, n % 3, :].rearrange("p (k n) -> p k n", k=4), src)\
                                .then_inc(landed[n % 3], 16)

            @block.scalar
            def _(act):
                def gate(c):
                    act.wait_ge(multiplied, R3 * c + 2)
                    if c >= 1:
                        act.wait_ge(joined, c)
                    act.activation(sg[:, :, :], acc[:, 0:NT, :], ACT.Sigmoid).then_inc(gated, 1)

                high_blocks(act, tp, yhi, NB * 4, turned, hi_done)
                for n in range(units):
                    act.wait_ge(landed[n % 3], 16 * (n // 3 + 1))
                    if n >= SPL:
                        act.wait_ge(multiplied, n - SPL + 1)
                    act.activation(b.whi[:, n % SPL, :], b.wraw[:, n % 3, :], ACT.Copy).then_inc(high, 1)
                    if n % R3 == 2:
                        gate(n // R3)

            @block.vector
            def _(dve):
                def join(c):
                    br, cc = c // 2, c % 2
                    dve.wait_ge(multiplied, R3 * c + 3)
                    dve.wait_ge(gated, c + 1)
                    m = b.mg[:, :, cc * 512:cc * 512 + 512]
                    if br == 0:
                        dve.tensor_tensor(m, acc[:, NT:2 * NT, :], sg[:, :, :], ALU.mult).then_inc(joined, 1)
                    else:
                        dve.tensor_tensor(sg[:, :, :], acc[:, NT:2 * NT, :], sg[:, :, :], ALU.mult).then_inc(merged, 1)
                        dve.wait_ge(merged, c - 1)
                        dve.wait_ge(joined, c)
                        dve.tensor_tensor(m, m, sg[:, :, :], ALU.add).then_inc(joined, 1)

                low_blocks(dve, tp, yhi, ylo, NB * 4, hi_done, lo_done)
                for n in range(units):
                    dve.wait_ge(high, n + 1)
                    dve.tensor_tensor(b.wlo[:, n % SPL, :], b.wraw[:, n % 3, :], b.whi[:, n % SPL, :].bitcast(F32),
                                      ALU.subtract).then_inc(split, 1)
                    if n % R3 == 0 and n >= R3:
                        join(n // R3 - 1)
                join(units // R3 - 1)

            @block.tensor
            def _(pe):
                turn_blocks(pe, b, tp, lambda t, n: b.y[:, t, n // 4, (n % 4) * P:(n % 4) * P + P], NB * 4,
                            turned, lo_done)
                pe.wait_ge(lo_done, NB * 4)
                for n in range(units):
                    c, j = n // R3, n % R3
                    if c >= 1 and j == 0:
                        pe.wait_ge(gated, c)
                    if c >= 1 and j == 2:
                        pe.wait_ge(joined, c)
                    pe.wait_ge(split, n + 1)
                    for k4 in range(4):
                        cs = slice(k4 * 512, k4 * 512 + 512)
                        for t in range(NT):
                            r = slice(t * P, t * P + P)
                            if j < 2:
                                k = 4 * j + k4
                                last = product(pe, acc[:, t, :], b.hhi[:, k, r], b.hlo[:, k, r],
                                               b.whi[:, n % SPL, cs], b.wlo[:, n % SPL, cs], k == 0, k == KD - 1)
                            else:
                                k = 4 * (c // 2) + k4
                                last = product(pe, acc[:, NT + t, :], yhi[:, k, r], ylo[:, k, r],
                                               b.whi[:, n % SPL, cs], b.wlo[:, n % SPL, cs], k4 == 0, k4 == 3)
                    last.then_inc(multiplied, 1)


def out_project(nc, b, a, l):
    w = at(l, a["w_out"]).rearrange("(q k p) n -> q p k n", p=P, k=4)
    with ExitStack() as ctx:
        acc = ctx.enter_context(psum(nc, "out_acc", [P, 2 * NT, 512], F32))
        tp = ctx.enter_context(psum(nc, "ps_merged", [P, 2, 512], F32))
        gx = ctx.enter_context(sbuf(nc, "gated_out", [P, 2, NT, 512], F32))
        with stage(nc, "landed0", "landed1", "landed2", "landed3", "high", "split", "multiplied", "gated", "added",
                   "turned", "hi_done", "lo_done") as (
                *landed, high, split, multiplied, gated, added, turned, hi_done, lo_done), nc.Block() as block:
            @block.sync
            def _(sp):
                for n in range(4):
                    sp.dma_start(b.wraw[:, n, :].rearrange("p (k n) -> p k n", k=4),
                                 w[n % 2][:, :, (n // 2) * 512:(n // 2) * 512 + 512]).then_inc(landed[n], 16)

            @block.scalar
            def _(act):
                high_blocks(act, tp, b.hhi, KD, turned, hi_done)
                for n in range(4):
                    act.wait_ge(landed[n], 16)
                    if n >= SPL:
                        act.wait_ge(multiplied, n - SPL + 1)
                    act.activation(b.whi[:, n % SPL, :], b.wraw[:, n, :], ACT.Copy).then_inc(high, 1)

            @block.vector
            def _(dve):
                def add(c):
                    cs = slice(c * 512, c * 512 + 512)
                    dve.wait_ge(multiplied, 2 * c + 2)
                    dve.tensor_tensor(gx[:, c, 0, :], acc[:, NT * c, :], b.gate[0][:, 0, cs], ALU.mult)\
                        .then_inc(gated, 1)
                    dve.tensor_tensor(gx[:, c, 1:3, :], acc[:, NT * c + 1:NT * c + 3, :],
                                      b.gate[0][:, 1, cs].unsqueeze(1).to_broadcast([P, 2, 512]), ALU.mult)\
                        .then_inc(gated, 1)
                    dve.wait_ge(gated, 2 * c + 2)
                    dve.tensor_tensor(b.x[:, :, cs], b.x[:, :, cs], gx[:, c], ALU.add).then_inc(added, 1)

                low_blocks(dve, tp, b.hhi, b.hlo, KD, hi_done, lo_done)
                for n in range(4):
                    dve.wait_ge(high, n + 1)
                    dve.tensor_tensor(b.wlo[:, n % SPL, :], b.wraw[:, n, :], b.whi[:, n % SPL, :].bitcast(F32),
                                      ALU.subtract).then_inc(split, 1)
                    if n == 2:
                        add(0)
                add(1)

            @block.tensor
            def _(pe):
                turn_blocks(pe, b, tp, lambda t, n: b.mg[:, t, n * P:n * P + P], KD, turned, lo_done)
                pe.wait_ge(lo_done, KD)
                for n in range(4):
                    pe.wait_ge(split, n + 1)
                    for k4 in range(4):
                        k = 4 * (n % 2) + k4
                        cs = slice(k4 * 512, k4 * 512 + 512)
                        for t in range(NT):
                            r = slice(t * P, t * P + P)
                            last = product(pe, acc[:, NT * (n // 2) + t, :], b.hhi[:, k, r], b.hlo[:, k, r],
                                           b.whi[:, n % SPL, cs], b.wlo[:, n % SPL, cs], k == 0, k == KD - 1)
                    last.then_inc(multiplied, 1)


def key_load(b, a, l, landed, sp, n):
    w = at(l, a["peer_wq"]).rearrange("(i k r) n -> i r k n", i=4, k=KD)
    for i in range(4):
        sp.dma_start(b.wraw[32 * i:32 * i + 32, n % RAW, :].rearrange("p (k n) -> p k n", k=KD),
                     w[i][:, :, n * 256:n * 256 + 256]).then_inc(landed[n % RAW], 16)


def key_scores(nc, b, a, l, landed):
    G = 2 * PH
    with ExitStack() as ctx:
        sb = lambda n, s, dt=F32: ctx.enter_context(sbuf(nc, n, s, dt))
        ps = lambda n, s: ctx.enter_context(psum(nc, n, s, F32))
        sk = sb("subkeys", [P, 2, P])
        skt = sb("subkeys_t", [P, 2, P])
        q = sb("queries", [P, 2, TOK])
        rest = sb("scores_rest", [P, NT, NK])
        tp = ps("ps_sk", [P, 512])
        pq = ps("ps_q", [P, 2, 512])
        pss = ps("ps_s", [P, 2, 512])
        with stage(nc, "keys_in", "k_turned", "k_copied",
                   "high", "split", "q_done", "q_copied", "scored", "picked", "dve_done", also=landed) as (
                keys_in, k_turned, k_copied, high, split, q_done, q_copied, scored, picked, dve_done), \
                nc.Block() as block:
            @block.sync
            def _(sp):
                sp.dma_start(sk[:, :, :], at(l, a["peer_subkeys"]).rearrange("s n d -> n s d")).then_inc(keys_in, 16)
                for n in range(RAW, PH):
                    sp.wait_ge(split, n - RAW + 1)
                    key_load(b, a, l, landed, sp, n)

            @block.gpsimd
            def _(pool):
                for n in range(PH):
                    pool.wait_ge(high, n + 1)
                    pool.tensor_tensor(b.wlo[:, n % SPL, :], b.wraw[:, n % RAW, :],
                                       b.whi[:, n % SPL, :].bitcast(F32), ALU.subtract).then_inc(split, 1)

            @block.scalar
            def _(act):
                def unit(n):
                    act.wait_ge(landed[n % RAW], 64 * (n // RAW + 1))
                    if n >= SPL:
                        act.wait_ge(q_done, 2 * (n - SPL) + 2)
                    act.activation(b.whi[:, n % SPL, :], b.wraw[:, n % RAW, :], ACT.Copy).then_inc(high, 1)

                unit(0)
                act.wait_ge(k_turned, 1)
                act.activation(skt[:, :, :].rearrange("p s n -> p (s n)"), tp[:, 0:256], ACT.Copy)\
                    .then_inc(k_copied, 1)
                for g in range(G):
                    if g % 2 == 0 and g // 2 + 1 < PH:
                        unit(g // 2 + 1)
                    act.wait_ge(q_done, g + 1)
                    if g >= 2:
                        act.wait_ge(scored, g - 1)
                    act.activation(q[:, g % 2, :], pq[:, g % 2, 0:TOK], ACT.Copy).then_inc(q_copied, 1)

            @block.vector
            def _(dve):
                link = Chain(dve, dve_done)
                for g in range(G):
                    s = [pss[:, g % 2, t * P:t * P + P] for t in range(NT)]
                    v, ix = b.best[:, :, g, :], b.index[:, :, g, :]
                    dve.wait_ge(scored, g + 1)
                    for t in range(NT):
                        last = dve.max(v[:, t, 0:8], s[t])
                    link(last)
                    for t in range(NT):
                        last = dve.max_index(ix[:, t, 0:8], v[:, t, 0:8], s[t])
                    for t in range(NT):
                        last = dve.match_replace(rest[:, t, :], v[:, t, 0:8], s[t], -3.0e38)
                    last.then_inc(picked, 1)
                    dve.wait_ge(picked, g + 1)
                    for t in range(NT):
                        last = dve.max(v[:, t, 8:16], rest[:, t, :])
                    link(last)
                    for t in range(NT):
                        last = dve.max_index(ix[:, t, 8:16], v[:, t, 8:16], rest[:, t, :])
                    link(last)

            @block.tensor
            def _(pe):
                def query(g):
                    pe.wait_ge(split, g // 2 + 1)
                    if g >= 2:
                        pe.wait_ge(q_copied, g - 1)
                    u = (g // 2) % SPL
                    for k in range(KD):
                        c = slice(k * 256 + (g % 2) * P, k * 256 + (g % 2) * P + P)
                        last = product(pe, pq[:, g % 2, 0:TOK], b.whi[:, u, c], b.wlo[:, u, c],
                                       b.hhi[:, k, :], b.hlo[:, k, :], k == 0, k == KD - 1)
                    last.then_inc(q_done, 1)

                def score(g):
                    pe.wait_ge(q_copied, g + 1)
                    pe.wait_ge(k_copied, 1)
                    if g >= 2:
                        pe.wait_ge(picked, g - 1)
                    for t in range(NT):
                        r = slice(t * P, t * P + P)
                        last = pe.matmul(pss[:, g % 2, r], q[:, g % 2, r], skt[:, g % 2, :], start=True, stop=True,
                                         skip_group_check=True)
                    last.then_inc(scored, 1)

                pe.wait_ge(keys_in, 16)
                for i in range(2):
                    last = pe.transpose(tp[:, i * P:i * P + P], sk[:, i, :], b.ident)
                last.then_inc(k_turned, 1)
                query(0)
                for g in range(1, G):
                    query(g)
                    score(g - 1)
                score(G - 1)


def choose(nc, b, a, nl):
    HH = NT * PH
    CHUNKS = MOD_CHUNKS - MOD_BESIDE
    wide = [P, SLOTS, TOPK]
    with ExitStack() as ctx:
        sb = lambda n, s, dt=F32: ctx.enter_context(sbuf(nc, n, s, dt))
        ixf = sb("key_index_f", [P, HH, 2, TOPK])
        d1 = sb("index_steps", [P, HH, TOPK])
        cand = sb("sums", [P, HH, NSUM])
        best = sb("best_sums", [P, HH, TOPK])
        pos = sb("best_pos", [P, HH, TOPK], U32)
        posf = sb("best_pos_f", [P, HH, TOPK])
        off = sb("best_column", [P, NT, SLOTS])
        code = sb("code", [P, NT, 2, SLOTS], U32)
        codef = sb("code_f", [P, NT, 3, SLOTS])
        ge = sb("row_reached", [P, SLOTS, TOPK])
        eq = sb("column_equal", [P, 2, SLOTS, TOPK])
        out = sb("slots", [P, NT, 3, SLOTS])
        e = sb("exps", [P, HH, TOPK])
        st = sb("gate_stats", [P, 2, HH])
        rows = sb("mod_rows", [2, 2, 512])
        acc = ctx.enter_context(psum(nc, "mod_acc", [P, 2, 512], F32))
        pt = ctx.enter_context(psum(nc, "ps_slots", [P, NT, 512], F32))
        with stage(nc, *[f"landed{j}" for j in range(RAW)], "used", "kept", "written0", "written1", "dve_done", "ask",
                   "expd", "compared", "picked", "ready", "turned", "slots_in") as (
                *landed, used, kept, written0, written1, dve_done, ask, expd, compared, picked, ready, turned,
                slots_in), nc.Block() as block:
            written = (written0, written1)

            @block.sync
            def _(sp):
                load_modulation(sp, b, a, nl, CHUNKS, landed, used)

            @block.tensor
            def _(pe):
                for chunk in range(CHUNKS):
                    multiply_modulation(pe, b, acc, chunk, landed, used, kept)
                for t in range(NT):
                    pe.wait_ge(ready, t + 1)
                    for i in range(3):
                        last = pe.transpose(pt[:, t, i * P:i * P + P], out[:, t, i, :], b.ident)
                    last.then_inc(turned, 1)

            @block.scalar
            def _(act):
                for chunk in range(CHUNKS):
                    keep_modulation(act, rows, acc, chunk, used, kept, written)
                    store_modulation(act, b, rows, chunk, kept, written)
                    if chunk == 3:
                        act.wait_ge(ask, 1)
                        act.activation(e[:, :, :], e[:, :, :], ACT.Exp).then_inc(expd, 1)
                for t in range(NT):
                    act.wait_ge(turned, t + 1)
                    r = slice(t * P, t * P + P)
                    src = pt[:, t, 0:3 * P].rearrange("p (i n) -> p i n", i=3)
                    act.activation(b.slots[:, 0:3, r], src, ACT.Copy).then_inc(slots_in, 1)
                    act.activation(b.slots[:, 3:5, r], src[:, 0:2], ACT.Copy, scale=-1.0).then_inc(slots_in, 1)
                for i in range(2):
                    act.wait_ge(written[i], 16 * ((CHUNKS + 1 - i) // 2))

            @block.gpsimd
            def _(pool):
                for t in range(NT):
                    pool.wait_ge(compared, t + 1)
                    by_head = eq[:, t % 2].rearrange("p (h k) j -> p h k j", h=PH)
                    pool.tensor_tensor(by_head, by_head, ixf[:, PH * t:PH * t + PH, 1, :].unsqueeze(2)
                                       .to_broadcast([P, PH, TOPK, TOPK]), ALU.mult).then_inc(picked, 1)

            @block.vector
            def _(dve):
                link = Chain(dve, dve_done)
                v = b.best[:, :, :, :].rearrange("p t (h s) n -> p (t h) s n", s=2)
                v1, v2 = v[:, :, 0, :], v[:, :, 1, :]
                for i in range(5):
                    n = ROWS[i]
                    last = dve.tensor_tensor(cand[:, :, STARTS[i]:STARTS[i] + n],
                                             v1[:, :, i:i + 1].to_broadcast([P, HH, n]), v2[:, :, 0:n], ALU.add)
                last = dve.tensor_tensor(cand[:, :, STARTS[5]:STARTS[8]].rearrange("p h (i j) -> p h i j", j=2),
                                         v1[:, :, 5:8].unsqueeze(3).to_broadcast([P, HH, 3, 2]),
                                         v2[:, :, 0:2].unsqueeze(2).to_broadcast([P, HH, 3, 2]), ALU.add)
                last = dve.tensor_tensor(cand[:, :, STARTS[8]:NSUM], v1[:, :, 8:16],
                                         v2[:, :, 0:1].to_broadcast([P, HH, 8]), ALU.add)
                link(last)
                for r in range(2):
                    o = slice(8 * r, 8 * r + 8)
                    for h in range(HH):
                        last = dve.max(best[:, h, o], cand[:, h, :])
                    link(last)
                    for h in range(HH):
                        last = dve.max_index(pos[:, h, o], best[:, h, o], cand[:, h, :])
                    link(last)
                    if r == 0:
                        for h in range(HH):
                            last = dve.match_replace(cand[:, h, :], best[:, h, o], cand[:, h, :], -3.0e38)
                        link(last)
                dve.tensor_tensor(e[:, :, :], best[:, :, :], best[:, :, 0:1].to_broadcast([P, HH, TOPK]),
                                  ALU.subtract).then_inc(ask, 1)
                dve.tensor_copy(ixf[:, :, :, :], b.index[:, :, :, :].rearrange("p t (h s) n -> p (t h) s n", s=2))
                link(dve.tensor_copy(posf[:, :, :], pos[:, :, :]))
                dve.tensor_copy(d1[:, :, 0:1], ixf[:, :, 0, 0:1])
                link(dve.tensor_tensor(d1[:, :, 1:TOPK], ixf[:, :, 0, 1:TOPK], ixf[:, :, 0, 0:TOPK - 1], ALU.subtract))
                link(dve.scalar_tensor_tensor(d1[:, :, :], d1[:, :, :], 64.0,
                                              b.cst[:, C_DS:C_DS + TOPK].unsqueeze(1).to_broadcast([P, HH, TOPK]),
                                              ALU.mult, ALU.add))

                def second_index(t):
                    dve.wait_ge(picked, t + 1)
                    dve.tensor_reduce(out[:, t, 2, :], eq[:, t % 2], AX_X, ALU.add).then_inc(ready, 1)

                for t in range(NT):
                    hs = slice(PH * t, PH * t + PH)
                    place = posf[:, hs, :].rearrange("p h k -> p (h k)")
                    link(dve.tensor_tensor(ge[:, :, :], place.unsqueeze(2).to_broadcast(wide),
                                           b.cst[:, C_ST:C_ST + TOPK].unsqueeze(1).to_broadcast(wide), ALU.is_ge))
                    by_head = ge[:, :, :].rearrange("p (h k) j -> p h k j", h=PH)
                    link(dve.tensor_tensor(by_head, by_head, d1[:, hs, :].unsqueeze(2)
                                           .to_broadcast([P, PH, TOPK, TOPK]), ALU.mult))
                    link(dve.tensor_reduce(codef[:, t, 0, :], ge[:, :, :], AX_X, ALU.add))
                    link(dve.tensor_copy(code[:, t, 0, :], codef[:, t, 0, :]))
                    link(dve.tensor_scalar(code[:, t, 1, :], code[:, t, 0, :], 63, None, ALU.bitwise_and))
                    link(dve.tensor_copy(codef[:, t, 1, :], code[:, t, 1, :]))
                    dve.tensor_tensor(off[:, t, :], place, codef[:, t, 1, :], ALU.subtract)
                    link(dve.tensor_tensor(codef[:, t, 2, :], codef[:, t, 0, :], codef[:, t, 1, :], ALU.subtract))
                    link(dve.tensor_scalar(out[:, t, 1, :], codef[:, t, 2, :], 1.0 / 64, None, ALU.mult))
                    dve.tensor_tensor(eq[:, t % 2], off[:, t, :].unsqueeze(2).to_broadcast(wide),
                                      b.cst[:, C_IO:C_IO + TOPK].unsqueeze(1).to_broadcast(wide), ALU.is_equal)\
                        .then_inc(compared, 1)
                    if t == 0:
                        dve.wait_ge(expd, 1)
                        link(dve.tensor_reduce(st[:, 0, :], e[:, :, :], AX_X, ALU.add))
                        link(dve.reciprocal(st[:, 1, :], st[:, 0, :]))
                        link(dve.tensor_tensor(out[:, :, 0, :].rearrange("p t (h k) -> p t h k", h=PH),
                                               e[:, :, :].rearrange("p (t h) k -> p t h k", t=NT),
                                               st[:, 1, :].rearrange("p (t h) -> p t h", t=NT).unsqueeze(3)
                                               .to_broadcast([P, NT, PH, TOPK]), ALU.mult))
                    else:
                        second_index(t - 1)
                second_index(NT - 1)


def spread_gates(nc, b, a, nl, gates_out, first_experts):
    GROUP = 4
    TG = P // GROUP
    NG = NT * TG
    OH2, OH1 = 3, 2
    SHARE = 4
    by_act = lambda g: g % SHARE == SHARE - 1
    own = lambda g: g - (g + 1) // SHARE
    beside = [0, 3, 6, 8, 11, 13, 16, 18, 21, 24, 27, 30] + [TG * t + g for t in (1, 2) for g in (18, 20, 23, 25, 28, 30)]
    assert len(beside) == MOD_BESIDE * KD
    first_chunk = MOD_CHUNKS - MOD_BESIDE
    with ExitStack() as ctx:
        sb = lambda n, s, dt=F32: ctx.enter_context(sbuf(nc, n, s, dt))
        gm = (sb("gates_tile", [P, NK, P]), b.gm1)
        away = sb("distance", [P, GROUP, NK])
        oh2 = sb("one_hot_2", [P, OH2, GROUP, NK])
        oh1 = sb("one_hot_1", [P, OH1, GROUP, NK])
        oha = sb("one_hot_1_act", [P, 2, GROUP, NK])
        w = sb("mod_weights", [P, 512])
        rows = sb("mod_row", [2, 512])
        acc = ctx.enter_context(psum(nc, "mod_acc", [P, 512], F32))
        ps = ctx.enter_context(psum(nc, "ps_gates", [P, 6, 512], F32))
        wm = at(nl, a["w_mod"]).rearrange("(k p) n -> p k n", p=P)
        with stage(nc, "landed", "used", "kept", "mods_out", "hot1", "hot1_act", "hot2", "spread", "summed",
                   "stored") as (landed, used, kept, mods_out, hot1, hot1_act, hot2, spread, summed,
                                 stored), nc.Block() as block:
            @block.sync
            def _(sp):
                def load(m):
                    if m:
                        sp.wait_ge(used, m)
                    c = (first_chunk + m // KD) * 512
                    sp.dma_start(w[:, :], wm[:, m % KD, c:c + 512]).then_inc(landed, 16)

                for t in range(NT):
                    for m, g in enumerate(beside):
                        if g // TG == t:
                            load(m)
                        if t == NT - 1 and g == beside[-1]:
                            for q in range(4):
                                sp.wait_ge(gates_out[q], 16 * 2)
                            first_experts(sp)
                    sp.wait_ge(stored, TG * (t + 1))
                    dst = b.gates[t].rearrange("i p n -> p i n")
                    for q in range(4):
                        sp.dma_start(dst[:, 32 * q:32 * q + 32, :], gm[t % 2][:, 32 * q:32 * q + 32, :])\
                            .then_inc(gates_out[q], 16)

            @block.tensor
            def _(pe):
                def modulate(m):
                    pe.wait_ge(landed, 16 * (m + 1))
                    if m % KD == 0 and m:
                        pe.wait_ge(kept, m // KD)
                    pe.matmul(acc[0:2, :], b.cnd[:, m % KD, :], w[:, :], start=(m % KD == 0), stop=(m % KD == KD - 1),
                              skip_group_check=True).then_inc(used, 1)

                for g in range(NG):
                    pe.wait_ge(hot2, g + 1)
                    if by_act(g):
                        pe.wait_ge(hot1_act, (g + 1) // SHARE)
                        first = oha[:, (g // SHARE) % 2]
                    else:
                        pe.wait_ge(hot1, own(g) + 1)
                        first = oh1[:, own(g) % OH1]
                    if g >= 6:
                        pe.wait_ge(stored, g - 5)
                    for i in range(GROUP):
                        last = pe.matmul(ps[:, g % 6, i * NK:i * NK + NK], first[:, i, :], oh2[:, g % OH2, i, :],
                                         start=True, stop=True, skip_group_check=True)
                    last.then_inc(summed, 1)
                    if g in beside:
                        modulate(beside.index(g))

            @block.scalar
            def _(act):
                iota = b.cst[:, C_IO:C_IO + NK]

                def hot(g):
                    j = g // SHARE
                    if j >= 2:
                        act.wait_ge(summed, g - 2 * SHARE + 1)
                    if j:
                        act.wait_ge(hot1_act, j)
                    for i in range(GROUP):
                        n = g * GROUP + i
                        last = act.activation(away[:, i, :], iota, ACT.Abs, bias=b.slots[:, 4, n:n + 1])
                    last.then_inc(spread, 1)
                    act.wait_ge(spread, j + 1)
                    for i in range(GROUP):
                        n = g * GROUP + i
                        last = act.activation(oha[:, j % 2, i, :], away[:, i, :], ACT.Relu,
                                              bias=b.slots[:, 0, n:n + 1], scale=b.slots[:, 3, n:n + 1])
                    last.then_inc(hot1_act, 1)

                def store(g):
                    t = g // TG
                    n = (g % TG) * GROUP
                    act.wait_ge(summed, g + 1)
                    if t >= 2 and g % TG == 0:
                        for q in range(4):
                            act.wait_ge(gates_out[q], 16 * (t - 1))
                    act.activation(gm[t % 2][:, :, n:n + GROUP].rearrange("p i n -> p n i"),
                                   ps[:, g % 6, :].rearrange("p (n i) -> p n i", n=GROUP), ACT.Copy)\
                        .then_inc(stored, 1)

                def keep(chunk):
                    act.wait_ge(used, KD * (chunk + 1))
                    if chunk:
                        act.wait_ge(mods_out, 16 * chunk)
                    act.activation(rows[:, :], acc[0:2, :], ACT.Copy).then_inc(kept, 1)
                    act.wait_ge(kept, chunk + 1)
                    c = (first_chunk + chunk) * 512
                    act.dma_start(b.mods[:, c:c + 512], rows[:, :]).then_inc(mods_out, 16)

                hot(SHARE - 1)
                for g in range(NG):
                    store(g)
                    if g % SHARE == 0 and g + 2 * SHARE - 1 < NG:
                        hot(g + 2 * SHARE - 1)
                    if g in beside[KD - 1::KD]:
                        keep(beside.index(g) // KD)
                act.wait_ge(mods_out, 16 * MOD_BESIDE)

            @block.vector
            def _(dve):
                iota = b.cst[:, C_IO:C_IO + NK]
                for g in range(NG):
                    if g >= OH2:
                        dve.wait_ge(summed, g - OH2 + 1)
                    n = g * GROUP
                    dve.tensor_tensor(oh2[:, g % OH2], iota.unsqueeze(1).to_broadcast([P, GROUP, NK]),
                                      b.slots[:, 2, n:n + GROUP].unsqueeze(2).to_broadcast([P, GROUP, NK]),
                                      ALU.is_equal).then_inc(hot2, 1)
                    if not by_act(g):
                        if own(g) >= OH1:
                            before = next(x for x in range(g) if own(x) == own(g) - OH1 and not by_act(x))
                            dve.wait_ge(summed, before + 1)
                        for i in range(GROUP):
                            last = dve.tensor_scalar(oh1[:, own(g) % OH1, i, :], iota, b.slots[:, 1, n + i:n + i + 1],
                                                     b.slots[:, 0, n + i:n + i + 1], ALU.is_equal, ALU.mult)
                        last.then_inc(hot1, 1)


def expert_rows(b):
    flat = b.gm1[:, :, :].rearrange("p i n -> p (i n)")
    return [flat[:, 2 * D * i:2 * D * i + 2 * D].rearrange("p (s d) -> p s d", s=2) for i in range(2)]


def load_u(b, a, l, eng, e, par, u_in):
    src = at(l, a["peer_u"]).rearrange("(m c e) (i n) -> e i c m n", e=NK, i=4, m=4)[bass.ds(e, 1)]
    src = src.rearrange("a i c m n -> (a i) c m n")
    u = expert_rows(b)[0]
    for i in range(4):
        eng.dma_start(u[32 * i:32 * i + 32, par, :].rearrange("p (m n) -> p m n", m=4), src[i]).then_inc(u_in[par], 16)


def load_v(b, a, l, eng, e, par, v_in):
    src = at(l, a["peer_v"]).rearrange("(p i) d -> i p d", i=NK)[bass.ds(e, 1)].rearrange("a p d -> (a p) d")
    eng.dma_start(expert_rows(b)[1][:, par, :], src).then_inc(v_in[par], 16)


def experts(nc, b, a, l, gates_out, u_in, v_in):
    E = NK
    GATES_OUT = 16 * NT
    gt = b.gates.rearrange("t i p n -> i p t n")
    with ExitStack() as ctx:
        sb = lambda n, s, dt=F32: ctx.enter_context(sbuf(nc, n, s, dt))
        ps = lambda n, s: ctx.enter_context(psum(nc, n, s, F32))
        u, v = expert_rows(b)
        flat = b.gm1[:, :, :].rearrange("p i n -> p (i n)")
        sizes = (2 * KD * P, 2 * TOK, 2 * TOK, 2 * TOK, NT * D)
        starts = [4 * D + sum(sizes[:i]) for i in range(5)]
        u_t, g, act_out, wt, gx = (flat[:, o:o + n] for o, n in zip(starts, sizes))
        u_t = u_t.rearrange("p (s n) -> p s n", s=2)
        g = g.rearrange("p (s t n) -> p s t n", s=2, t=NT)
        act_out, wt = (x.rearrange("p (s n) -> p s n", s=2) for x in (act_out, wt))
        gx = gx.rearrange("p (t n) -> p t n", t=NT)
        vhi, vlo = sb("v_hi", [P, 2, D], F32R), sb("v_lo", [P, 2, D], F32R)
        whi, wlo = sb("w_hi", [P, 2, TOK], F32R), sb("w_lo", [P, 2, TOK], F32R)
        sb("quarters_going_out", [P, NK * P - 4 * D - 4 * TOK])
        uhi, ulo = sb("u_hi", [P, 2, KD * P], F32R), sb("u_lo", [P, 2, KD * P], F32R)
        acc = ps("expert_acc", [P, NT * 2, 512])
        pa = ps("ps_act", [P, 512])
        with stage(nc, "g_in0", "g_in1", "u_turned", "u_high", "u_low", "scored", "gelu_done", "weighed", "w_high",
                   "w_low", "v_high", "v_low", "summed", "gated", "added", also=[*u_in, *v_in]) as (
                g_in0, g_in1, u_turned, u_high, u_low, scored, gelu_done, weighed, w_high, w_low, v_high, v_low,
                summed, gated, added), nc.Block() as block:
            g_in = (g_in0, g_in1)

            @block.sync
            def _(sp):
                with sp.Fori(1, E // 2) as pair:
                    for par in range(2):
                        e = pair * 2 + par
                        sp.wait_ge(u_turned, e - 1)
                        load_u(b, a, l, sp, e, par, u_in)
                        sp.wait_ge(v_low, e - 1)
                        load_v(b, a, l, sp, e, par, v_in)

            def landed_count(e, par, per):
                return (e // 2 + 1) * per if isinstance(e, int) else (e - par) * (per // 2) + per

            @block.scalar
            def _(act):
                def u_part(e, par, first):
                    act.wait_ge(u_turned, e + 1)
                    if not first:
                        act.wait_ge(scored, e - 1)
                    act.activation(uhi[:, par, :], u_t[:, par, :], ACT.Copy).then_inc(u_high, 1)

                def v_part(e, par, first):
                    act.wait_ge(v_in[par], landed_count(e, par, 16))
                    if not first:
                        act.wait_ge(summed, e - 1)
                    act.activation(vhi[:, par, :], v[:, par, :], ACT.Copy).then_inc(v_high, 1)

                def load_gates(e, par):
                    act.dma_start(g[:, par], gt[bass.ds(e, 1)].rearrange("a p t n -> (a p) t n")).then_inc(g_in[par], 16)

                def step(e, par, first, last, load_next=True):
                    if not last:
                        u_part(e + 1, 1 - par, first and par == 0)
                    v_part(e, par, first)
                    act.wait_ge(scored, e + 1)
                    act.activation(act_out[:, par, :], pa[:, 0:TOK], ACT.Gelu_apprx_tanh).then_inc(gelu_done, 1)
                    act.wait_ge(weighed, e + 1)
                    if first and par == 0:
                        act.wait_ge(gates_out[1], GATES_OUT)
                    act.activation(whi[:, par, :], wt[:, par, :], ACT.Copy).then_inc(w_high, 1)
                    if load_next:
                        load_gates(e + 2, par)

                u_part(0, 0, True)
                act.wait_ge(gates_out[0], GATES_OUT)
                load_gates(0, 0)
                load_gates(1, 1)
                step(0, 0, True, False)
                step(1, 1, True, False)
                for q in range(2, 4):
                    act.wait_ge(gates_out[q], GATES_OUT)
                with act.Fori(1, E // 2 - 1) as pair:
                    e = pair * 2
                    step(e, 0, False, False)
                    step(e + 1, 1, False, False)
                step(E - 2, 0, False, False, False)
                step(E - 1, 1, False, True, False)

            @block.vector
            def _(dve):
                def turn(e, par, first):
                    dve.wait_ge(u_in[par], landed_count(e, par, 64))
                    if not first:
                        dve.wait_ge(u_low, e - 1)
                    dve.transpose(u_t[:, par, :].rearrange("p (k m c) -> p m k c", m=4, c=32),
                                  u[:, par, :].rearrange("p (m k c) -> p m k c", m=4, c=32)).then_inc(u_turned, 1)

                def u_rest(e, par):
                    dve.wait_ge(u_high, e + 1)
                    dve.tensor_tensor(ulo[:, par, :], u_t[:, par, :], uhi[:, par, :].bitcast(F32), ALU.subtract)\
                        .then_inc(u_low, 1)

                def step(e, par, turn_next, last):
                    if not last:
                        u_rest(e + 1, 1 - par)
                    dve.wait_ge(v_high, e + 1)
                    dve.tensor_tensor(vlo[:, par, :], v[:, par, :], vhi[:, par, :].bitcast(F32), ALU.subtract)\
                        .then_inc(v_low, 1)
                    dve.wait_ge(gelu_done, e + 1)
                    dve.wait_ge(g_in[par], landed_count(e, par, 16))
                    dve.tensor_tensor(wt[:, par, :], act_out[:, par, :], g[:, par].rearrange("p t n -> p (t n)"),
                                      ALU.mult).then_inc(weighed, 1)
                    dve.wait_ge(w_high, e + 1)
                    dve.tensor_tensor(wlo[:, par, :], wt[:, par, :], whi[:, par, :].bitcast(F32), ALU.subtract)\
                        .then_inc(w_low, 1)
                    if turn_next:
                        turn(e + 2, par, False)

                turn(0, 0, True)
                turn(1, 1, True)
                u_rest(0, 0)
                with dve.Fori(0, E // 2 - 1) as pair:
                    e = pair * 2
                    step(e, 0, True, False)
                    step(e + 1, 1, True, False)
                step(E - 2, 0, False, False)
                step(E - 1, 1, False, True)
                dve.wait_ge(summed, E)
                dve.tensor_tensor(gx[:, 0, :], acc[:, 0:2, :].rearrange("p c n -> p (c n)"), b.gate[1][:, 0, :],
                                  ALU.mult).then_inc(gated, 1)
                dve.tensor_tensor(gx[:, 1:3, :], acc[:, 2:6, :].rearrange("p (t c) n -> p t (c n)", c=2),
                                  b.gate[1][:, 1, :].unsqueeze(1).to_broadcast([P, 2, D]), ALU.mult).then_inc(gated, 1)
                dve.wait_ge(gated, 2)
                dve.tensor_tensor(b.x[:, :, :], b.x[:, :, :], gx[:, :, :], ALU.add).then_inc(added, 1)

            @block.tensor
            def _(pe):
                def score(e, par, first):
                    pe.wait_ge(u_low, e + 1)
                    if not first:
                        pe.wait_ge(gelu_done, e)
                    for k in range(KD):
                        c = slice(k * P, k * P + P)
                        last = product(pe, pa[:, 0:TOK], uhi[:, par, c], ulo[:, par, c], b.hhi[:, k, :],
                                       b.hlo[:, k, :], k == 0, k == KD - 1)
                    last.then_inc(scored, 1)

                def add(e, par, first):
                    pe.wait_ge(w_low, e + 1)
                    for t in range(NT):
                        r = slice(t * P, t * P + P)
                        for c in range(2):
                            cs = slice(c * 512, c * 512 + 512)
                            last = product(pe, acc[:, 2 * t + c, :], whi[:, par, r], wlo[:, par, r],
                                           vhi[:, par, cs], vlo[:, par, cs], first, False)
                    last.then_inc(summed, 1)

                score(0, 0, True)
                score(1, 1, False)
                add(0, 0, True)
                with pe.Fori(1, E // 2) as pair:
                    e = pair * 2
                    for d in range(2):
                        score(e + d, d, False)
                        add(e + (d - 1), 1 - d, False)
                add(E - 1, 1, False)


def final(nc, b, a):
    with ExitStack() as ctx:
        gf = ctx.enter_context(sbuf(nc, "final_gain", [P, D], F32))
        y = ctx.enter_context(sbuf(nc, "final_out", [P, NT, D], F32))
        st = ctx.enter_context(sbuf(nc, "final_stats", [P, 4, NT], F32))
        with stage(nc, "loaded", "squared", "dve_done", "rooted", "normed", "written") as (
                loaded, squared, dve_done, rooted, normed, written), nc.Block() as block:
            @block.sync
            def _(sp):
                sp.dma_start(gf[:, :], a["norm_f"].partition_broadcast(P)).then_inc(loaded, 16)
                sp.wait_ge(normed, NT)
                sp.dma_start(a["o_prompt"][0], y[:, 0, :]).then_inc(written, 16)
                sp.dma_start(a["o_sample"][0].rearrange("(t p) d -> p t d", p=P), y[:, 1:3, :]).then_inc(written, 16)
                sp.wait_ge(written, 32)

            @block.scalar
            def _(act):
                for t in range(NT):
                    act.activation(y[:, t, :], b.x[:, t, :], ACT.Square, accum_out=st[:, 0, t:t + 1])\
                        .then_inc(squared, 1)
                act.wait_ge(dve_done, 1)
                act.activation(st[:, 2, :], st[:, 1, :], ACT.Sqrt).then_inc(rooted, 1)

            @block.vector
            def _(dve):
                link = Chain(dve, dve_done)
                dve.wait_ge(squared, NT)
                link(dve.tensor_scalar(st[:, 1, :], st[:, 0, :], 1.0 / D, EPS, ALU.mult, ALU.add))
                dve.wait_ge(rooted, 1)
                link(dve.reciprocal(st[:, 3, :], st[:, 2, :]))
                dve.wait_ge(loaded, 16)
                for t in range(NT):
                    dve.scalar_tensor_tensor(y[:, t, :], b.x[:, t, :], st[:, 3, t:t + 1], gf[:, :],
                                             ALU.mult, ALU.mult).then_inc(normed, 1)


def program(nc, a):
    with ExitStack() as ctx:
        def sb(name, shape, dt=F32):
            return ctx.enter_context(sbuf(nc, name, shape, dt))

        b = Buffers()
        b.x = sb("x", [P, NT, D])
        b.cst = sb("cst", [P, C_ALL])
        b.ident = b.cst[:, C_ID:C_ID + P]
        b.cnd = sb("conditions", [P, KD, 2])
        b.hhi, b.hlo = sb("h_hi", [P, KD, TOK], F32R), sb("h_lo", [P, KD, TOK], F32R)
        b.scale, b.shift = sb("scale", [P, 2, KD, 2]), sb("shift", [P, 2, KD, 2])
        b.gate = [None, sb("gate_2", [P, 2, D])]
        b.bias = nc.dram_tensor("bias_scratch", (DEPTH, P, 2, H, LAT), F32, kind="Internal").ap()
        b.mods = nc.dram_tensor("mod_scratch", (2, 6 * D), F32, kind="Internal").ap()
        b.gates = nc.dram_tensor("gate_scratch", (NT, NK, P, P), F32, kind="Internal").ap()

        @contextmanager
        def stream():
            with sbuf(nc, "w_raw", [P, RAW, UNIT], F32) as b.wraw, \
                    sbuf(nc, "w_high", [P, SPL, UNIT], F32R) as b.whi, \
                    sbuf(nc, "w_low", [P, SPL, UNIT], F32R) as b.wlo:
                yield

        with sbuf(nc, "w_raw", [P, RAW, UNIT]) as b.wraw:
            setup(nc, b, a)
        with nc.Fori(0, DEPTH) as l:
            with sbuf(nc, "gate_1", [P, 2, D]) as b.gate[0], sbuf(nc, "y", [P, NT, NB, BW]) as b.y, \
                    sbuf(nc, "log_gamma", [P, 8]) as b.lg, sbuf(nc, "log_gamma_pairs", [P, 2, H // 2]) as b.lgp:
                with sbuf(nc, "proj", [P, NT, MIX_W]) as b.proj:
                    with stream(), early(nc) as landed:
                        norm(nc, b, a, l, 0, lambda sp: [project_load(b, a, l, landed, sp, 0, j) for j in range(RAW)],
                             b.proj[:, :, :].rearrange("p t n -> p (t n)"))
                        project(nc, b, a, l, landed)
                    attention(nc, b, a, l)
                    retention(nc, b, a, l)
                with sbuf(nc, "merged", [P, NT, D]) as b.mg, stream():
                    merge(nc, b, a, l)
                    out_project(nc, b, a, l)
            with stage(nc, "gates_out0", "gates_out1", "gates_out2", "gates_out3") as gates_out:
                with sbuf(nc, "slots_t", [P, 5, TOK]) as b.slots:
                    with sbuf(nc, "best_keys", [P, NT, 2 * PH, TOPK]) as b.best, \
                            sbuf(nc, "key_index", [P, NT, 2 * PH, TOPK], U32) as b.index:
                        with stream(), early(nc) as landed:
                            norm(nc, b, a, l, 1, lambda sp: [key_load(b, a, l, landed, sp, n) for n in range(RAW)])
                            key_scores(nc, b, a, l, landed)
                        with sbuf(nc, "w_raw", [P, RAW, UNIT]) as b.wraw:
                            choose(nc, b, a, (l + 1) % DEPTH)
                    with sbuf(nc, "gates_tile_1", [P, NK, P]) as b.gm1, early(nc) as (*u_in, v_in0, v_in1):
                        v_in = (v_in0, v_in1)

                        def first_experts(sp):
                            for par in range(2):
                                load_u(b, a, l, sp, par, par, u_in)
                                load_v(b, a, l, sp, par, par, v_in)

                        spread_gates(nc, b, a, (l + 1) % DEPTH, gates_out, first_experts)
                        experts(nc, b, a, l, gates_out, u_in, v_in)
        final(nc, b, a)


INPUTS = ["x_prompt", "x_sample", "c", "cache_diff_k", "cache_diff_v", "cache_na_k", "cache_na_v", "state_ret",
          "c_ctx", "w_mod", "b_mod", "norm1", "w_in", "diff_lambda", "diff_gn", "ret_decay", "ret_gn", "na_pad",
          "w_branch", "w_out", "norm2", "peer_wq", "peer_subkeys", "peer_u", "peer_v", "norm_f"]
OUTPUTS = [("o_prompt", (1, CTX, D)), ("o_sample", (1, LAT, D)),
           ("o_diff_k", (1, DEPTH, H, CTX, DH)), ("o_diff_v", (1, DEPTH, H, CTX, DH)),
           ("o_na_k", (1, DEPTH, H, CTX, DH)), ("o_na_v", (1, DEPTH, H, CTX, DH)),
           ("o_state", (1, DEPTH, 2, H, 64, DH))]


def kernel(**inputs):
    import concourse.bacc as bacc
    from concourse.bass_utils import run_bass_kernel_spmd

    inputs["na_pad"] = np.pad(np.asarray(inputs["na_bias"]), ((0, 0), (0, 0), (0, 0), (48, 48)))
    nc = bacc.Bacc("TRN2", target_bir_lowering=False, num_devices=1)
    arrays, a = {}, {}
    for name in INPUTS:
        v = np.ascontiguousarray(inputs[name])
        arrays[name + "_in"] = v
        a[name] = nc.dram_tensor(name + "_in", v.shape, mybir.dt.from_np(v.dtype), kind="ExternalInput").ap()
    for name, shape in OUTPUTS:
        a[name] = nc.dram_tensor(name, shape, F32, kind="ExternalOutput").ap()
    a["const"] = nc.inline_tensor(constants(), name="constants").ap()
    program(nc, a)
    r = run_bass_kernel_spmd(nc, [arrays], core_ids=[0])
    return tuple(r.results[0][name] for name, _ in OUTPUTS)
```
